# Optimizing a Trainium2 kernel written in Bass

```python
import math
import jax, jax.numpy as jnp
from jax import lax
import numpy as np

D_MODEL = 1024
BATCH = 1
SEQ = 128
DEPTH = 2
DEC_BATCH = 1
DEC_SEQ = 512
PAST_LEN = 256

GRID_W = 64
N_HEADS_A = 4
HEAD_DIM_A = 64
A_QK = N_HEADS_A * HEAD_DIM_A
A_V = N_HEADS_A * 2 * HEAD_DIM_A
D_INNER_B = D_MODEL // 2
HEAD_DIM_B = 64
N_HEADS_B = D_INNER_B // HEAD_DIM_B
N_GROUPS_B = 2
D_STATE = 128
D_CONV = 5
CONV_DIM_B = D_INNER_B + 2 * N_GROUPS_B * D_STATE
CHUNK = 128
W_IN0 = 4 * A_QK + A_V + D_INNER_B + CONV_DIM_B + 2 * N_HEADS_B
POOL_WINDOWS = (2, 4, 8, 16)
N_POOL_GROUPS = 4
POOL_GROUP_DIM = D_MODEL // N_POOL_GROUPS
D_FF = 4 * D_MODEL
N_MOD = 6
ROPE_BASE = 10000.0
LN_EPS = 1e-5
ALPHA = (2 * DEPTH) ** 0.25
BETA = (8 * DEPTH) ** -0.25

kernel_name = "diffattn_ssd_pool_prefix_dit_step"

def layer_norm(x, g, b):
    xf = x.astype(jnp.float32)
    mu = jnp.mean(xf, -1, keepdims=True)
    var = jnp.mean(jnp.square(xf - mu), -1, keepdims=True)
    return ((xf - mu) * lax.rsqrt(var + LN_EPS) * g + b).astype(x.dtype)

def rms_norm(x, w, eps=1e-5):
    xf = x.astype(jnp.float32)
    return (xf * lax.rsqrt(jnp.mean(xf * xf, -1, keepdims=True) + eps) * w).astype(x.dtype)

def modulation(cond, w_mod, b_mod):
    m = jax.nn.silu(cond) @ w_mod + b_mod
    return jnp.split(m[..., None, :], N_MOD, axis=-1)

def modulate(x, shift, scale):
    return x * (1 + scale) + shift

def axial_rope_tables(rows):
    r, col = jnp.meshgrid(jnp.arange(rows), jnp.arange(GRID_W), indexing="ij")
    r = r.reshape(-1).astype(jnp.float32)
    col = col.reshape(-1).astype(jnp.float32)
    n_freq = HEAD_DIM_A // 4
    inv = ROPE_BASE ** (-jnp.arange(n_freq, dtype=jnp.float32) / n_freq)
    ang = jnp.concatenate([r[:, None] * inv, col[:, None] * inv], -1)
    return jnp.cos(ang), jnp.sin(ang)

def apply_rope(x, cos, sin):
    half = x.shape[-1] // 2
    x1 = x[..., :half].astype(jnp.float32)
    x2 = x[..., half:].astype(jnp.float32)
    c = cos[None, :, None, :]
    s = sin[None, :, None, :]
    return jnp.concatenate([x1 * c - x2 * s, x2 * c + x1 * s], -1).astype(x.dtype)

def diff_attention(q1, q2, k1, k2, v, lam):
    nb, lq, h, d = q1.shape
    qb = math.gcd(lq, 128)
    nblk = lq // qb
    scale = d ** -0.5
    f32 = jnp.float32
    k1f, k2f, vf = k1.astype(f32), k2.astype(f32), v.astype(f32)

    def blocks(q):
        return jnp.moveaxis(q.reshape(nb, nblk, qb, h, d), 1, 0)

    def one_block(qs):
        qa, qc = qs
        s1 = jnp.einsum('bqhd,bkhd->bhqk', qa.astype(f32) * scale, k1f)
        s2 = jnp.einsum('bqhd,bkhd->bhqk', qc.astype(f32) * scale, k2f)
        p = jax.nn.softmax(s1, axis=-1) - lam * jax.nn.softmax(s2, axis=-1)
        return jnp.einsum('bhqk,bkhe->bqhe', p, vf)

    out = lax.map(one_block, (blocks(q1), blocks(q2)))
    return jnp.moveaxis(out, 0, 1).reshape(nb, lq, h, 2 * d).astype(v.dtype)

def centred_dwconv(x, w, bias):
    pad = D_CONV // 2
    y = lax.conv_general_dilated(x, w[:, None, :].astype(x.dtype), window_strides=(1,),
                                 padding=[(pad, pad)], dimension_numbers=('NWC', 'WIO', 'NWC'),
                                 feature_group_count=x.shape[-1])
    return y + bias

def ssd_scan(x, dt, a, bmat, cmat, h0):
    f32 = jnp.float32
    nb, L, H, P = x.shape
    q = math.gcd(L, CHUNK)
    nc = L // q
    rep = H // N_GROUPS_B
    bh = jnp.repeat(bmat.astype(f32), rep, axis=2).reshape(nb, nc, q, H, D_STATE)
    ch = jnp.repeat(cmat.astype(f32), rep, axis=2).reshape(nb, nc, q, H, D_STATE)
    xdt = (x.astype(f32) * dt[..., None]).reshape(nb, nc, q, H, P)
    acs = jnp.cumsum((dt * a).reshape(nb, nc, q, H), axis=2)
    seg = acs[:, :, :, None, :] - acs[:, :, None, :, :]
    causal = jnp.tril(jnp.ones((q, q), bool))[None, None, :, :, None]
    decay = jnp.where(causal, jnp.exp(jnp.where(causal, seg, 0.0)), 0.0)
    cb = jnp.einsum('bclhn,bcshn->bclsh', ch, bh) * decay
    y_diag = jnp.einsum('bclsh,bcshp->bclhp', cb, xdt)
    decay_to_end = jnp.exp(acs[:, :, -1:, :] - acs)
    chunk_states = jnp.einsum('bclhn,bclh,bclhp->bchpn', bh, decay_to_end, xdt)
    chunk_decay = jnp.exp(acs[:, :, -1, :])

    def step(hs, inp):
        st, dec = inp
        return hs * dec[:, :, None, None] + st, hs

    h_final, h_enter = lax.scan(step, h0.astype(f32),
                                (jnp.moveaxis(chunk_states, 1, 0), jnp.moveaxis(chunk_decay, 1, 0)))
    h_enter = jnp.moveaxis(h_enter, 0, 1)
    y_off = jnp.einsum('bclhn,bchpn,bclh->bclhp', ch, h_enter, jnp.exp(acs))
    return (y_diag + y_off).reshape(nb, L, H, P), h_final

def bidir_ssd(x, dt_f, dt_b, a_f, a_b, bm, cm, h0_f, h0_b):
    y_f, hf = ssd_scan(x, dt_f, a_f, bm, cm, h0_f)
    flip = lambda t: jnp.flip(t, axis=1)
    y_b, hb = ssd_scan(flip(x), flip(dt_b), a_b, flip(bm), flip(cm), h0_b)
    return y_f + flip(y_b), hf, hb

def ab_mixer(h, p, lam, lam_init, ctx, rope):
    f32 = jnp.float32
    nb, L, _ = h.shape
    u = h @ p["w_in"]
    sizes = (A_QK, A_QK, A_QK, A_QK, A_V, D_INNER_B, CONV_DIM_B)
    cuts = [int(s) for s in np.cumsum(sizes)]
    q1, q2, k1, k2, v, z, xbc, dt = jnp.split(u, cuts, axis=-1)
    q1, q2, k1, k2 = (t.reshape(nb, L, N_HEADS_A, HEAD_DIM_A) for t in (q1, q2, k1, k2))
    v = v.reshape(nb, L, N_HEADS_A, 2 * HEAD_DIM_A)
    if rope is not None:
        cos, sin = rope
        q1, q2, k1, k2 = (apply_rope(t, cos, sin) for t in (q1, q2, k1, k2))
    k_new = jnp.stack([k1, k2], axis=2)
    if ctx is None:
        k_all, v_all = k_new, v
        h0 = jnp.zeros((nb, 2, N_HEADS_B, HEAD_DIM_B, D_STATE), f32)
    else:
        cache_k, cache_v, state = ctx
        k_all = jnp.concatenate([cache_k.astype(k_new.dtype), k_new], axis=1)
        v_all = jnp.concatenate([cache_v.astype(v.dtype), v], axis=1)
        h0 = state
    o_a = diff_attention(q1, q2, k_all[:, :, 0], k_all[:, :, 1], v_all, lam)
    o_a = rms_norm(o_a, p["subln_w"]) * (1.0 - lam_init)
    xbc = jax.nn.silu(centred_dwconv(xbc, p["conv_w"], p["conv_b"]))
    xs, bm, cm = jnp.split(xbc, [D_INNER_B, D_INNER_B + N_GROUPS_B * D_STATE], axis=-1)
    xs = xs.reshape(nb, L, N_HEADS_B, HEAD_DIM_B)
    bm = bm.reshape(nb, L, N_GROUPS_B, D_STATE)
    cm = cm.reshape(nb, L, N_GROUPS_B, D_STATE)
    dt = jax.nn.softplus(dt.astype(f32) + p["dt_bias"].reshape(-1).astype(f32))
    a = -jnp.exp(p["a_log"].astype(f32))
    y, hf, hb = bidir_ssd(xs, dt[..., :N_HEADS_B], dt[..., N_HEADS_B:], a[0], a[1],
                          bm, cm, h0[:, 0], h0[:, 1])
    y = y + p["d_skip"][:, None] * xs
    y = rms_norm(y.reshape(nb, L, D_INNER_B) * jax.nn.silu(z), p["ssm_norm_w"])
    out = jnp.concatenate([o_a.reshape(nb, L, A_V), y.astype(h.dtype)], axis=-1) @ p["w_out"]
    return out, (k_new, v, jnp.stack([hf, hb], axis=1))

def multiscale_pool(u):
    f32 = jnp.float32
    nb, L, _ = u.shape
    uf = u.astype(f32)
    csum = jnp.pad(jnp.cumsum(uf, axis=1), ((0, 0), (1, 0), (0, 0)))
    t = jnp.arange(L)
    outs = []
    for g, w in enumerate(POOL_WINDOWS):
        lo = jnp.clip(t - w // 2, 0, L)
        hi = jnp.clip(t + w - w // 2, 0, L)
        sl = slice(g * POOL_GROUP_DIM, (g + 1) * POOL_GROUP_DIM)
        cs = csum[..., sl]
        mean = (cs[:, hi] - cs[:, lo]) / (hi - lo).astype(f32)[None, :, None]
        outs.append(mean - uf[..., sl])
    return jnp.concatenate(outs, axis=-1)

def pool_mixer(h, p):
    nb, L, _ = h.shape
    u = h @ p["w_in"]
    pooled = multiscale_pool(u).reshape(nb, L, N_POOL_GROUPS, POOL_GROUP_DIM)
    mixed = jnp.einsum('blgc,gce->blge', pooled, p["pool_w"].astype(jnp.float32))
    mixed = mixed.reshape(nb, L, D_MODEL).astype(h.dtype) * p["pool_scale"]
    return mixed @ p["w_out"]

def sq_relu_mlp(h, w_up, w_down):
    return jnp.square(jax.nn.relu(h @ w_up)) @ w_down

def setup_inputs(seed: int = 0) -> dict:
    key = jax.random.key(seed)
    keys = iter(jax.random.split(key, 64))
    f32 = jnp.float32

    def nrm(shape, s=1.0):
        return jax.random.normal(next(keys), shape, f32) * s

    def gain(shape):
        return 1.0 + nrm(shape, 0.05)

    def dt_bias(shape):
        u = jax.random.uniform(next(keys), shape, f32)
        dt = jnp.exp(u * (math.log(1e-1) - math.log(1e-3)) + math.log(1e-3))
        return dt + jnp.log(-jnp.expm1(-dt))

    inp = {}
    inp["x_prompt"] = nrm((BATCH, SEQ, D_MODEL))
    inp["x_sample"] = nrm((DEC_BATCH, DEC_SEQ, D_MODEL))
    inp["cache_k_l0"] = nrm((DEC_BATCH, PAST_LEN, 2, N_HEADS_A, HEAD_DIM_A))
    inp["cache_v_l0"] = nrm((DEC_BATCH, PAST_LEN, N_HEADS_A, 2 * HEAD_DIM_A))
    inp["state_ssm_l0"] = nrm((DEC_BATCH, 2, N_HEADS_B, HEAD_DIM_B, D_STATE))
    inp["c"] = nrm((DEC_BATCH, D_MODEL))
    inp["c_ctx"] = nrm((D_MODEL,))
    s_d = D_MODEL ** -0.5
    inp["w_mod_l0"] = nrm((D_MODEL, N_MOD * D_MODEL), 0.5 * s_d)
    inp["b_mod_l0"] = nrm((N_MOD * D_MODEL,), 0.01)
    inp["w_in_l0"] = nrm((D_MODEL, W_IN0), s_d)
    inp["conv_w_l0"] = nrm((D_CONV, CONV_DIM_B), D_CONV ** -0.5)
    inp["conv_b_l0"] = nrm((CONV_DIM_B,), 0.01)
    inp["a_log_l0"] = jnp.log(jax.random.uniform(next(keys), (2, N_HEADS_B), f32, 1.0, 16.0))
    inp["dt_bias_l0"] = dt_bias((2, N_HEADS_B))
    inp["d_skip_l0"] = gain((N_HEADS_B,))
    inp["ssm_norm_w_l0"] = gain((D_INNER_B,))
    inp["lam_q1_l0"] = nrm((HEAD_DIM_A,), 0.1)
    inp["lam_k1_l0"] = nrm((HEAD_DIM_A,), 0.1)
    inp["lam_q2_l0"] = nrm((HEAD_DIM_A,), 0.1)
    inp["lam_k2_l0"] = nrm((HEAD_DIM_A,), 0.1)
    inp["subln_w_l0"] = gain((2 * HEAD_DIM_A,))
    inp["w_out_l0"] = nrm((A_V + D_INNER_B, D_MODEL), BETA * (A_V + D_INNER_B) ** -0.5)
    inp["ln1_g_l0"] = gain((D_MODEL,))
    inp["ln1_b_l0"] = nrm((D_MODEL,), 0.01)
    inp["w_up_l0"] = nrm((D_MODEL, D_FF), s_d)
    inp["w_down_l0"] = nrm((D_FF, D_MODEL), BETA * D_FF ** -0.5)
    inp["ln2_g_l0"] = gain((D_MODEL,))
    inp["ln2_b_l0"] = nrm((D_MODEL,), 0.01)
    inp["w_mod_l1"] = nrm((D_MODEL, N_MOD * D_MODEL), 0.5 * s_d)
    inp["b_mod_l1"] = nrm((N_MOD * D_MODEL,), 0.01)
    inp["w_in_l1"] = nrm((D_MODEL, D_MODEL), s_d)
    inp["pool_w_l1"] = nrm((N_POOL_GROUPS, POOL_GROUP_DIM, POOL_GROUP_DIM), POOL_GROUP_DIM ** -0.5)
    inp["pool_scale_l1"] = gain((D_MODEL,))
    inp["w_out_l1"] = nrm((D_MODEL, D_MODEL), BETA * s_d)
    inp["ln1_g_l1"] = gain((D_MODEL,))
    inp["ln1_b_l1"] = nrm((D_MODEL,), 0.01)
    inp["w_up_l1"] = nrm((D_MODEL, D_FF), s_d)
    inp["w_down_l1"] = nrm((D_FF, D_MODEL), BETA * D_FF ** -0.5)
    inp["ln2_g_l1"] = gain((D_MODEL,))
    inp["ln2_b_l1"] = nrm((D_MODEL,), 0.01)
    return inp

def reference(x_prompt, x_sample, cache_k_l0, cache_v_l0, state_ssm_l0, c, c_ctx,
              w_mod_l0, b_mod_l0, w_in_l0, conv_w_l0, conv_b_l0, a_log_l0, dt_bias_l0,
              d_skip_l0, ssm_norm_w_l0, lam_q1_l0, lam_k1_l0, lam_q2_l0, lam_k2_l0,
              subln_w_l0, w_out_l0, ln1_g_l0, ln1_b_l0, w_up_l0, w_down_l0, ln2_g_l0, ln2_b_l0,
              w_mod_l1, b_mod_l1, w_in_l1, pool_w_l1, pool_scale_l1, w_out_l1,
              ln1_g_l1, ln1_b_l1, w_up_l1, w_down_l1, ln2_g_l1, ln2_b_l1):
    layers = (
        dict(w_mod=w_mod_l0, b_mod=b_mod_l0, w_in=w_in_l0, conv_w=conv_w_l0, conv_b=conv_b_l0,
             a_log=a_log_l0, dt_bias=dt_bias_l0, d_skip=d_skip_l0, ssm_norm_w=ssm_norm_w_l0,
             lam_q1=lam_q1_l0, lam_k1=lam_k1_l0, lam_q2=lam_q2_l0, lam_k2=lam_k2_l0,
             subln_w=subln_w_l0, w_out=w_out_l0, ln1_g=ln1_g_l0, ln1_b=ln1_b_l0,
             w_up=w_up_l0, w_down=w_down_l0, ln2_g=ln2_g_l0, ln2_b=ln2_b_l0,
             cache_k=cache_k_l0, cache_v=cache_v_l0, state_ssm=state_ssm_l0),
        dict(w_mod=w_mod_l1, b_mod=b_mod_l1, w_in=w_in_l1, pool_w=pool_w_l1,
             pool_scale=pool_scale_l1, w_out=w_out_l1, ln1_g=ln1_g_l1, ln1_b=ln1_b_l1,
             w_up=w_up_l1, w_down=w_down_l1, ln2_g=ln2_g_l1, ln2_b=ln2_b_l1),
    )
    rows = x_sample.shape[1] // GRID_W
    rope = axial_rope_tables(rows)
    xc, xl = x_prompt, x_sample
    for l in range(DEPTH):
        p = layers[l]
        mc = modulation(c_ctx, p["w_mod"], p["b_mod"])
        ml = modulation(c, p["w_mod"], p["b_mod"])
        hc = modulate(xc, mc[0], mc[1])
        hl = modulate(xl, ml[0], ml[1])
        if l % 2 == 0:
            lam_init = 0.8 - 0.6 * math.exp(-0.3 * l)
            lam = (jnp.exp(jnp.sum(p["lam_q1"] * p["lam_k1"]))
                   - jnp.exp(jnp.sum(p["lam_q2"] * p["lam_k2"]))).astype(jnp.float32) + lam_init
            dc, ctx_tensors = ab_mixer(hc, p, lam, lam_init, None, None)
            dl, _ = ab_mixer(hl, p, lam, lam_init, (p["cache_k"], p["cache_v"], p["state_ssm"]), rope)
            new_k_l0, new_v_l0, new_ssm_l0 = ctx_tensors
        else:
            dc = pool_mixer(hc, p)
            dl = pool_mixer(hl, p)
        xc = layer_norm(ALPHA * xc + mc[2] * dc, p["ln1_g"], p["ln1_b"])
        xl = layer_norm(ALPHA * xl + ml[2] * dl, p["ln1_g"], p["ln1_b"])
        fc = sq_relu_mlp(modulate(xc, mc[3], mc[4]), p["w_up"], p["w_down"])
        fl = sq_relu_mlp(modulate(xl, ml[3], ml[4]), p["w_up"], p["w_down"])
        xc = layer_norm(ALPHA * xc + mc[5] * fc, p["ln2_g"], p["ln2_b"])
        xl = layer_norm(ALPHA * xl + ml[5] * fl, p["ln2_g"], p["ln2_b"])
    return (xc, xl, new_k_l0, new_v_l0, new_ssm_l0)


_drawn_inputs = setup_inputs


def setup_inputs(seed=0):
    import zlib

    import numpy as np

    out = dict(_drawn_inputs(seed))
    spreads = {}
    factors = {'cache_k_l0': 5.484,
     'cache_v_l0': 4.673,
     'conv_b_l0': 3.308,
     'd_skip_l0': 24.492,
     'ssm_norm_w_l0': 27.512,
     'lam_q1_l0': 8.0,
     'lam_k1_l0': 3.087,
     'lam_q2_l0': 8.0,
     'lam_k2_l0': 8.0,
     'subln_w_l0': 23.839,
     'ln1_b_l0': 5.835,
     'ln2_b_l0': 6.187,
     'b_mod_l1': 8.0,
     'pool_scale_l1': 8.0,
     'ln1_b_l1': 5.86,
     'ln2_b_l1': 5.47}
    for name, (base, spread) in spreads.items():
        noise = np.random.default_rng([zlib.crc32(name.encode()), seed]).standard_normal(out[name].shape)
        drawn = base * np.exp(spread * noise) if base else spread * noise
        out[name] = __import__('jax').numpy.asarray(drawn.astype(out[name].dtype))
    for name, factor in factors.items():
        out[name] = (out[name] * factor).astype(out[name].dtype)
    return out
```

```python
import math
from contextlib import ExitStack

import numpy as np
import concourse.bass as bass
from concourse import mybir

F32 = mybir.dt.float32
F32R = mybir.dt.float32r
ALU = mybir.AluOpType
ACT = mybir.ActivationFunctionType
AX = mybir.AxisListType

P = 128
D = 1024
KT = D // P
NT = 5
LAT = 4
TOK = NT * P
HALF = TOK // 2
FF = 4096
BW = 256
BLK = KT * BW
CHUNK = 512
NCHUNK = FF // CHUNK
NH_A, DH = 4, 64
NH_B = 8
PAST = 256
KEYS = PAST + LAT * P
EPS = 1e-5
ALPHA = (2 * 2) ** 0.25
SCALE = DH ** -0.5
GRID_W = 64
ROPE_BASE = 10000.0
POOL_W = (2, 4, 8, 16)
LAM_INIT = 0.8 - 0.6 * math.exp(-0.3 * 0)
C_XBC, C_Z, C_V, C_DT = 2048, 1536, 1024, 3072
PADW = 8 + 512 + 8 + 8 + 128 + 8
SEG = ((8, 0, 512), (8 + 512 + 8 + 8, 512, 128))
CSEG = ((2, 0, 512), (518, 512, 128))
CPAD = 648
NEG = -1e30
ORDER = [4, 0, 1, 2, 3]
NA = NT * NH_A


def shape_tables():
    i = np.arange(P)
    ident = np.eye(P, dtype=np.float32)
    upto = (i[:, None] <= i[None, :]).astype(np.float32)
    frm = (i[:, None] >= i[None, :]).astype(np.float32)
    mask_f = np.where(upto > 0, 0.0, NEG).astype(np.float32)
    mask_b = np.where(frm > 0, 0.0, NEG).astype(np.float32)
    sel = np.zeros((P, 2, P), np.float32)
    for c in range(2):
        sel[c::32, c, :] = 1.0
    head = np.concatenate([ident, sel.reshape(P, -1)], 1)
    ssd = np.concatenate([upto, frm, mask_f, mask_b], 1)
    t = np.arange(LAT * P)
    inv = (np.float32(ROPE_BASE) ** (-np.arange(DH // 4, dtype=np.float32) / np.float32(DH // 4))).astype(np.float32)
    ang = np.concatenate([(t // GRID_W).astype(np.float32)[:, None] * inv,
                          (t % GRID_W).astype(np.float32)[:, None] * inv], -1)
    cos = np.cos(ang).astype(np.float32).reshape(LAT, P, DH // 2)
    sin = np.sin(ang).astype(np.float32).reshape(LAT, P, DH // 2)
    rope = np.stack([cos, sin], 0).transpose(2, 1, 0, 3).reshape(P, -1)
    icnt = np.zeros((4, PADW), np.float32)
    for g, w in enumerate(POOL_W):
        for pos, _, n in SEG:
            tt = np.arange(n)
            lo, hi = np.clip(tt - w // 2, 0, n), np.clip(tt + w - w // 2, 0, n)
            icnt[g, pos:pos + n] = np.float32(1.0) / (hi - lo).astype(np.float32)
    return (np.ascontiguousarray(head), np.ascontiguousarray(ssd),
            np.ascontiguousarray(rope.astype(np.float32)), icnt)


def weight_stream():
    s = [("mod", 0, b) for b in range(8)]
    s += [("in", 0, C_XBC + BW * j) for j in range(4)]
    s += [("in", 0, c) for c in (C_V, C_V + BW, C_Z, C_Z + BW, 0, BW, 2 * BW, 3 * BW)]
    s += [("mod", 0, b) for b in range(8, 20)]
    s += [("mod", 1, b) for b in list(range(0, 8)) + list(range(12, 20))]
    s += [("mod", 0, b) for b in range(20, 24)]
    for layer in range(2):
        if layer == 1:
            s += [("in", 1, BW * j) for j in range(4)] + [("pool", 1, 0)]
            s += [("mod", 1, b) for b in list(range(8, 12)) + list(range(20, 24))]
        s += [("out", layer, BW * j) for j in range(4)]
        s += [("up", layer, 0), ("up", layer, 1)]
        for c in range(NCHUNK - 1):
            s += [("up", layer, 2 * (c + 1)), ("up", layer, 2 * (c + 1) + 1)]
            s += [("down", layer, 2 * c), ("down", layer, 2 * c + 1)]
        s += [("down", layer, 2 * NCHUNK - 2), ("down", layer, 2 * NCHUNK - 1)]
    return s


def build(nc, A, O):
    S = weight_stream()
    NS = len(S)
    w_ord = []
    m_ord = []
    nw = nm = 0
    for kind, _, _ in S:
        w_ord.append(nw)
        m_ord.append(nm)
        if kind == "mod":
            nm += 1
        else:
            nw += 1
    mod_k = [k for k in range(NS) if S[k][0] == "mod"]
    w_k = [k for k in range(NS) if S[k][0] != "mod"]
    W_OUT = [w_ord[next(k for k in range(NS) if S[k][:2] == ("out", l))] for l in range(2)]
    W_UP = [w_ord[next(k for k in range(NS) if S[k][:2] == ("up", l))] for l in range(2)]
    W_IN1 = w_ord[next(k for k in range(NS) if S[k][:2] == ("in", 1))]
    gate_blocks = [m for m, k in enumerate(mod_k) if (S[k][2] // 4) % 3 == 2]

    ctx = ExitStack()
    with ctx:
        base = (nc.sbuf_base + 31) // 32 * 32
        ctx.enter_context(nc.sbuf_tensor("arena", [P, 212832 // 4], F32))
        KB = 1024

        def at(name, kb, shape, dt=F32):
            n = 4
            for d in shape[1:]:
                n *= d
            assert kb * KB + n <= 212800, name
            return nc.alloc_sbuf_tensor_at(name, shape, dt, offset=base + int(kb * KB))

        def sem(name):
            return ctx.enter_context(nc.semaphore(name))

        raw = at("raw", 0, [P, 2, BLK])
        whi = at("whi", 16, [P, 2, BLK], F32R)
        wlo = at("wlo", 32, [P, 2, BLK], F32R)
        x = at("x_tok", 48, [P, NT, D])
        hhi = at("h_hi", 68, [P, KT, TOK], F32R)
        hlo = at("h_lo", 88, [P, KT, TOK], F32R)
        uhi = at("hid_hi", 108, [P, KT, TOK], F32R)
        ulo = at("hid_lo", 128, [P, KT, TOK], F32R)
        acc = at("acc", 148, [P, NT, D])
        gate = at("gate", 168, [P, 2, 2, D])
        gb = at("ln_gb", 184, [P, 2, D])
        tmp = at("tmp", 192, [P, 2, D])
        head = at("head", 200, [P, 3 * P])
        ident = head[:, 0:P]
        cpad = at("cpad", 201.5, [P, KT, 32])
        vecT = at("vecT", 202.5, [P, 72])
        bmodT = at("bmodT", 202.8125, [P, 96])
        modT = at("modT", 203.1875, [P, 2, 4, 8, 2])
        modrow = at("modrow", 203.6875, [P, 2, BW])
        gbias = at("gbias", 205.6875, [P, BW])
        smisc = at("smisc", 206.6875, [P, 104])
        st = smisc[:, 64:88].rearrange("p (s n) -> p s n", s=2)
        mv = smisc[:, 88:92].rearrange("p (s n) -> p s n", s=2)
        rs = smisc[:, 92:94].rearrange("p (s n) -> p s n", s=2)
        nlam = smisc[:, 0:1]
        lsum = smisc[:, 2:4]
        lexp = smisc[:, 4:6]
        halfp = smisc[:, 8:16]
        red = smisc[:, 96:104].rearrange("p (s n) -> p s n", s=2)
        mx = smisc[:, 20:24].rearrange("p (s n) -> p s n", s=2)
        nmx = smisc[:, 24:28].rearrange("p (s n) -> p s n", s=2)
        esum = smisc[:, 28:32].rearrange("p (s n) -> p s n", s=2)
        rec = smisc[:, 32:36].rearrange("p (s n) -> p s n", s=2)
        ss = smisc[:, 36:44].rearrange("p (s n) -> p s n", s=2)
        rr = smisc[:, 44:52].rearrange("p (s n) -> p s n", s=2)
        ysq = smisc[:, 52:54]
        yrs = smisc[:, 54:56]
        vec_rows = at("vec_rows", 184, [P, 2, P])
        thc = at("thc", 186, [P, 2, 16])
        lamv = at("lamv", 187, [P, 4, DH])
        xT = at("xT", 148, [P, KT, TOK])
        convT = at("convT", 148, [P, KT, TOK])
        qT = at("qT", 108, [P, 4, TOK])
        kT = at("kT", 118, [P, 4, KEYS])
        kTp = at("kTp", 130, [P, 4, P])
        v = at("v_tok", 132, [P, 7, 512])
        zs = at("z_tok", 176, [P, NT, 512])
        craw = at("conv_raw", 186, [P, 2, CPAD])
        wdt = at("wdt", 168, [P, KT, 16])
        wdth = at("wdt_hi", 168.5, [P, KT, 16], F32R)
        wdtl = at("wdt_lo", 169, [P, KT, 16], F32R)
        dtT = at("dtT", 169.5, [16, TOK])
        daT = at("daT", 172, [16, TOK])
        dta, dtb, dtc, dtd = (at(f"dt_{n}", 176 + 2.5 * j, [16, TOK]) for j, n in enumerate("abcd"))
        rp = at("rope_t", 146, [P, LAT, 2, DH // 2])
        db = at("dt_vec", 147, [16, 4])
        qk = tmp[:, 0, 0:512].rearrange("p (s n) -> p s n", s=2)
        ra = tmp[:, 0, 512:768]
        rb = tmp[:, 0, 768:1024]
        zth = tmp[:, 1, 0:512].rearrange("p (s n) -> p s n", s=2)
        knew = tmp[:, 1, 512:1024].rearrange("p (s n) -> p s n", s=2)
        xb = at("xb_tok", 68, [P, NT, 768])
        ef = at("e_f", 83, [P, NH_B, P])
        eb = at("e_b", 87, [P, NH_B, P])
        kc = at("kc", 83, [P, 2, 2, 4, DH])
        hst = at("h_state", 91, [P, 2, 512])
        wst = at("w_state", 95, [P, 2, 512])
        sld = at("state_ld", 99, [P, 2, 4, P])
        sm = at("ssd_small", 103, [P, 768])
        dtok = sm[:, 0:80].rearrange("p (t d h) -> p t d h", t=5, d=2)
        datok = sm[:, 80:160].rearrange("p (t d h) -> p t d h", t=5, d=2)
        acs = sm[:, 160:240].rearrange("p (d t h) -> p d t h", d=2, t=5)
        rend = sm[:, 240:320].rearrange("p (d t h) -> p d t h", d=2, t=5)
        eacs = sm[:, 320:400].rearrange("p (d t h) -> p d t h", d=2, t=5)
        dtw = sm[:, 400:480].rearrange("p (d t h) -> p d t h", d=2, t=5)
        cdec = sm[:, 480:560].rearrange("p (d t h) -> p d t h", d=2, t=5)
        ssdc = at("ssd_c", 106, [P, 4, P])
        y = at("y_tok", 148, [P, NT, 512])
        e = at("e_att", 16, [P, 2, 2, KEYS])
        pt = at("pT", 28, [P, 2, 6, P])
        oa = at("o_tok", 158, [P, NT, 512])
        normw = at("normw", 44, [P, 512])
        subw = at("subw", 46, [P, P])
        dsk = at("dsk", 46.5, [P, NH_B])
        sso = at("ssm_out", 34, [P, 2, 4, P])
        osq = at("osq", 38, [P, 512])
        yt = at("yt", 40, [P, 512])
        ub = at("u_pad", 148, [P, 2, PADW])
        pb = at("p_pad", 148 + 2 * PADW * 4 / KB, [P, 3, PADW])
        ic = at("icnt", 148 + 5 * PADW * 4 / KB, [P, 2, PADW])

        ps = ctx.enter_context(nc.psum_tensor("ps", [P, 8 * 512], F32))

        def bank(b, lo=0, hi=512):
            return ps[:, b * 512 + lo:b * 512 + hi]

        def two(b, n=HALF):
            return ps[:, b * 512:(b + 2) * 512].rearrange("p (b n) -> p b n", b=2)[:, :, 0:n]

        raw_ld = [sem("raw_ld0"), sem("raw_ld1")]
        hi_done, lo_done = sem("hi_done"), sem("lo_done")
        mod_main, mod_row, mod_tr, mod_out = sem("mod_main"), sem("mod_row"), sem("mod_tr"), sem("mod_out")
        gbias_ld = sem("gbias_ld")
        ld_head, ld_vec, ld_lam, ld_small, ld_mix, ld_ssd = (sem(n) for n in
            ("ld_head", "ld_vec", "ld_lam", "ld_small", "ld_mix", "ld_ssd"))
        x_ld = [sem(f"x_ld{t}") for t in range(NT)]
        cz, vec_tr, vec_cp, c_th, c_ok = sem("cpad_zero"), sem("vec_tr"), sem("vec_cp"), sem("c_th"), sem("c_ok")
        lam_s, lam_e, hp_ok = sem("lam_s"), sem("lam_e"), sem("halfp_ok")
        xT_tr, xT_ev = sem("xT_tr"), sem("xT_ev")
        h_md, h_hi, h_lo = sem("h_md"), sem("h_hi0"), sem("h_lo0")
        cpz, xb_mm, xb_ev, cv_v, cv_th, cv_ok = (sem(n) for n in
            ("conv_zero", "xb_mm", "xb_ev", "cv_v", "cv_th", "cv_ok"))
        dt_w, dt_wl, dt_mm, dt_x, dt_e, dt_u, dt_l, dt_ok = (sem(n) for n in
            ("dt_w", "dt_wl", "dt_mm", "dt_x", "dt_e", "dt_u", "dt_l", "dt_ok"))
        ib_mm, ib_z, ib_ev, qk_rd, qk_tr, qk_ev = (sem(n) for n in
            ("ib_mm", "ib_z", "ib_ev", "qk_rd", "qk_tr", "qk_ev"))
        xt_tr, xt_ev, dtr, dtk, acs_mm, acs_ok, kc_tr, kc_ev, sld_tr, hst_ok = (sem(n) for n in
            ("xt_tr", "xt_ev", "dt_tr", "dt_tok", "acs_mm", "acs_ok", "kc_tr", "kc_ev", "sld_tr", "hst_ok"))
        r_mm, g_mm, seg_ok, eexp, m_ok, yd_mm, y_ok = (sem(n) for n in
            ("r_mm", "g_mm", "seg_ok", "e_exp", "m_ok", "yd_mm", "y_ok"))
        dec_s, dec_e, dec_ok, w_ok, off_mm, st_mm, off_ok, h_ok = (sem(n) for n in
            ("dec_s", "dec_e", "dec_ok", "ws_ok", "off_mm", "st_mm", "off_ok", "hs_ok"))
        nst_tr, nst_ev, yg_ok, yg_sq, yg_rs, yn_ok = (sem(n) for n in
            ("nst_tr", "nst_ev", "yg_ok", "yg_sq", "yg_rs", "yn_ok"))
        s_mm, mx_ok, ex_ok, p_ok, pt_tr, pt_ev, pv_mm, o_sq, o_rs, o_ok = (sem(n) for n in
            ("s_mm", "mx_ok", "ex_ok", "p_ok", "pt_tr", "pt_ev", "pv_mm", "o_sq", "o_rs", "o_ok"))
        mix_tr, mix_hi, mix_lo = sem("mix_tr"), sem("mix_hi"), sem("mix_lo")
        out_mm = [sem(f"out_mm{l}") for l in range(2)]
        out_ev = [sem(f"out_ev{l}") for l in range(2)]
        up_mm = [sem(f"up_mm{l}") for l in range(2)]
        relu_ok = [sem(f"relu_ok{l}") for l in range(2)]
        sq_hi = [sem(f"sq_hi{l}") for l in range(2)]
        sq_f = [sem(f"sq_f{l}") for l in range(2)]
        sq_lo = [sem(f"sq_lo{l}") for l in range(2)]
        dn_mm = [sem(f"dn_mm{l}") for l in range(2)]
        acc_ok = [sem(f"acc_ok{l}") for l in range(2)]
        gb_ld = sem("gb_ld")
        ln_z, ln_st, ln_rs, ln_n, ln_g, ln_x, ln_tr, ln_ma, ln_md, ln_hi, ln_lo = (sem(n) for n in
            ("ln_z", "ln_stat", "ln_rsd", "ln_n", "ln_g", "ln_x", "ln_tr", "ln_ma", "ln_md", "ln_hi", "ln_lo"))
        Z_BASE = [0, 4 * NT, 6 * NT, 10 * NT]
        up_z, u_mm, u_ev, pl_f, pl_hi, pl_lo, px_mm, px_f, px_hi, px_lo = (sem(n) for n in
            ("u_zero", "u_mm", "u_ev", "pl_f", "pl_hi", "pl_lo", "px_mm", "px_f", "px_hi", "px_lo"))
        ic_ld = [sem("ic_ld0"), sem("ic_ld1")]
        vs, ss_ = sem("dve_step"), sem("pool_step")
        fin, fin2 = sem("stores"), sem("stores_pool")

        (x_prompt, x_sample, cache_k, cache_v, state_ssm, c_in, c_ctx) = (
            A[n] for n in ("x_prompt", "x_sample", "cache_k_l0", "cache_v_l0", "state_ssm_l0", "c", "c_ctx"))
        y_prompt, y_sample, new_k, new_v, new_ssm = O

        def mlp_steps(eng):
            seq = [("up", 0), ("up", 1)]
            for c in range(NCHUNK - 1):
                seq += [("up", 2 * c + 2), ("up", 2 * c + 3), ("down", 2 * c), ("down", 2 * c + 1)]
            seq += [("down", 2 * NCHUNK - 2), ("down", 2 * NCHUNK - 1)]
            for kind, n in seq[:PRE]:
                yield kind, n, None
            with eng.Fori(0, 2) as i:
                for kind, n in seq[PRE:PRE + BODY]:
                    yield kind, n, i
            for kind, n in seq[PRE + 2 * BODY:]:
                yield kind, n, None

        def raw_ready(eng, k, i=None):
            v_ = 16 * (k // 2 + 1)
            eng.wait_ge(raw_ld[k % 2], v_ if i is None else i * 64 + v_)

        def lin(v_, per, i):
            return v_ if i is None else i * per + v_

        K_UP = [next(k for k in range(NS) if S[k][:2] == ("up", l)) for l in range(2)]

        def read_by_pe(w):
            kind, layer, i = S[w_k[w]]
            if kind == "in":
                if layer == 1:
                    return u_mm, 2 * (w - W_IN1) + 2, 0
                return (xb_mm, 2 * w + 2, 0) if w < 4 else (ib_mm, 5 * (w - 3), 0)
            if kind == "out":
                return out_mm[layer], 5 * (w - W_OUT[layer]) + 5, 0
            if kind == "pool":
                return px_mm, KT, 0
            if kind == "up":
                return up_mm[layer], 2 * i + 2, 8
            return dn_mm[layer], 5 * i + 5, 20

        PRE, BODY = 10, 8
        SITES = 28
        M_MIX = 8

        block = ctx.enter_context(nc.Block())

        @block.sync
        def _(sp):
            def load(k, i=None):
                j = k - 2
                if j >= 0 and S[j][0] == "mod":
                    sp.wait_ge(mod_main, m_ord[j] + 1)
                elif j >= 0:
                    sp.wait_ge(lo_done, lin(w_ord[j] + 1, 8, i))
                kind, layer, n = S[k]
                if kind == "up":
                    c0 = n * BW if i is None else bass.ds(i * (4 * BW) + n * BW, BW)
                    src = A[f"w_up_l{layer}"][:, slice(c0, c0 + BW) if i is None else c0]
                elif kind == "down":
                    r0 = (n // 2) * CHUNK
                    rows = slice(r0, r0 + CHUNK) if i is None else bass.ds(i * (2 * CHUNK) + r0, CHUNK)
                    src = A[f"w_down_l{layer}"][rows, (n % 2) * 512:(n % 2) * 512 + 512]
                elif kind == "pool":
                    src = A["pool_w_l1"].rearrange("g k n -> (g k) n")
                elif kind == "mod":
                    src = A[f"w_mod_l{layer}"][:, n * BW:(n + 1) * BW]
                else:
                    src = A[f"w_{kind}_l{layer}"][:, n:n + BW]
                src = src.rearrange("(k p) n -> p k n", p=P)
                sp.dma_start(raw[:, k % 2, :].rearrange("p (k n) -> p k n", n=src.shape[2]), src) \
                    .then_inc(raw_ld[k % 2], 16)

            sp.dma_start(head[:], A["t_head"]).then_inc(ld_head, 16)
            sp.dma_start(vec_rows[0:8, 0, :], A["c"].rearrange("a (k p) -> (a k) p", p=P)).then_inc(ld_vec, 16)
            sp.dma_start(vec_rows[8:16, 0, :], A["c_ctx"].rearrange("(k p) -> k p", p=P)).then_inc(ld_vec, 16)
            sp.dma_start(vec_rows[16:56, 0, :], A["conv_w_l0"].rearrange("j (k p) -> (j k) p", p=P)).then_inc(ld_vec, 16)
            sp.dma_start(vec_rows[56:64, 0, :], A["conv_b_l0"].rearrange("(k p) -> k p", p=P)).then_inc(ld_vec, 16)
            sp.dma_start(vec_rows[64:72, 0, :], A["pool_scale_l1"].rearrange("(k p) -> k p", p=P)).then_inc(ld_vec, 16)
            for l in range(2):
                sp.dma_start(vec_rows[48 * l:48 * l + 48, 1, :],
                             A[f"b_mod_l{l}"].rearrange("(k p) -> k p", p=P)).then_inc(ld_vec, 16)
            k = 0
            for layer in range(2):
                while k < K_UP[layer] + PRE:
                    load(k)
                    k += 1
                with sp.Fori(0, 2) as i:
                    for j in range(BODY):
                        load(k + j, i)
                k += 2 * BODY
            while k < NS:
                load(k)
                k += 1
            for t in range(NT):
                sp.wait_ge(ln_x, 3 * NT + t + 1)
                dst = y_sample[0, t * P:(t + 1) * P, :] if t < LAT else y_prompt[0]
                sp.dma_start(dst, x[:, t, :]).then_inc(fin, 16)
            sp.wait_ge(fin, 16 * NT)

        @block.gpsimd
        def _(pool):
            pool.memset(cpad[:], 0.0).then_inc(cz, 1)
            pool.memset(halfp, -0.5).then_inc(hp_ok, 1)
            for n, name in enumerate(("lam_q1_l0", "lam_k1_l0", "lam_q2_l0", "lam_k2_l0")):
                pool.dma_start(lamv[:, n, :], A[name].partition_broadcast(P)).then_inc(ld_lam, 16)
            pool.dma_start(wdt[:], A["w_in_l0"][:, C_DT:C_DT + 16].rearrange("(k p) n -> p k n", p=P)).then_inc(ld_small, 16)
            pool.dma_start(db[:, 0:1], A["dt_bias_l0"].rearrange("a (h o) -> (a h) o", o=1)).then_inc(ld_small, 16)
            pool.dma_start(db[:, 1:2], A["a_log_l0"].rearrange("a (h o) -> (a h) o", o=1)).then_inc(ld_small, 16)
            pool.dma_start(rp[:], A["t_rope"].rearrange("p (t a f) -> p t a f", t=LAT, a=2)).then_inc(ld_small, 16)
            for tt in range(2):
                pool.dma_start(v[:, tt, :], cache_v[0, tt * P:(tt + 1) * P].rearrange("l h e -> l (h e)")) \
                    .then_inc(ld_small, 16)

            def gate_bias(n):
                if n >= 1:
                    pool.wait_ge(mod_out, gate_blocks[n - 1] + 1)
                _, layer, b = S[mod_k[gate_blocks[n]]]
                pool.dma_start(gbias[:], A[f"b_mod_l{layer}"][b * BW:(b + 1) * BW].partition_broadcast(P)) \
                    .then_inc(gbias_ld, 16)

            steps = [0]
            pool.wait_ge(hp_ok, 1)

            def rsqrt(dst, src, n, scale, done):
                pool.tensor_scalar(dst, src, scale, EPS, ALU.mult, ALU.add).then_inc(ss_, 1)
                steps[0] += 1
                pool.wait_ge(ss_, steps[0])
                pool.tensor_tensor(dst, dst, halfp[:, 0:n], ALU.pow).then_inc(done, 1)

            pool.wait_ge(c_ok, 1)
            pool.wait_ge(lam_s, 2)
            pool.memset(craw[:], 0.0).then_inc(cpz, 1)
            gate_bias(0)
            pool.wait_ge(ib_mm, 40)
            pool.dma_start(ssdc[:], A["t_ssd"].rearrange("p (a n) -> p a n", a=4)).then_inc(ld_mix, 16)
            pool.dma_start(normw[:], A["ssm_norm_w_l0"].partition_broadcast(P)).then_inc(ld_mix, 16)
            pool.dma_start(subw[:], A["subln_w_l0"].partition_broadcast(P)).then_inc(ld_mix, 16)
            pool.dma_start(dsk[:], A["d_skip_l0"].partition_broadcast(P)).then_inc(ld_mix, 16)
            for tt in range(2):
                src = cache_k[0, tt * P:(tt + 1) * P]
                pool.dma_start(kc[:, tt, 0, :, :], src[:, 0]).then_inc(ld_mix, 16)
                for h in range(NH_A):
                    pool.dma_start(kc[:, tt, 1, h ^ 1, :], src[:, 1, h, :]).then_inc(ld_mix, 16)
            for d in range(2):
                pool.dma_start(sld[:, d], state_ssm[0, d].rearrange("(r a) p n -> (a p) r n", a=2)).then_inc(ld_mix, 16)
            pool.wait_ge(ib_ev, 40)
            for n in range(2):
                pool.dma_start(new_k[0, :, n].rearrange("l h e -> l (h e)"), knew[:, n, :]).then_inc(fin2, 16)
            pool.dma_start(new_v[0].rearrange("l h e -> l (h e)"), v[:, 6, :]).then_inc(fin2, 16)
            for n in range(1, 4):
                gate_bias(n)
            pool.wait_ge(nst_ev, 2)
            for d in range(2):
                pool.dma_start(new_ssm[0, d].rearrange("(r a) p n -> (a p) r n", a=2), sso[:, d]).then_inc(fin2, 16)
            for t in range(NT):
                pool.wait_ge(yg_sq, t + 1)
                if t >= 2:
                    pool.wait_ge(yn_ok, t - 1)
                rsqrt(yrs[:, t % 2:t % 2 + 1], ysq[:, t % 2:t % 2 + 1], 1, 1.0 / 512, yg_rs)
            for t in range(NT):
                pool.wait_ge(o_sq, t + 1)
                if t >= 2:
                    pool.wait_ge(o_ok, t - 1)
                rsqrt(rr[:, t % 2, :], ss[:, t % 2, :], 4, 1.0 / 128, o_rs)

            def load_gb(i):
                layer, half = i // 2, i % 2
                if i > 0:
                    pool.wait_ge(ln_x, NT * i)
                for n, which in enumerate("gb"):
                    pool.dma_start(gb[:, n, :], A[f"ln{half + 1}_{which}_l{layer}"].partition_broadcast(P)) \
                        .then_inc(gb_ld, 16)

            def norm_share(i):
                for s in range(NT + 1):
                    if s < NT:
                        pool.wait_ge(ln_st, NT * i + s + 1)
                        if s >= 2:
                            pool.wait_ge(ln_n, NT * i + s - 1)
                        rsqrt(rs[:, s % 2, :], mv[:, s % 2, 1:2], 1, 1.0, ln_rs)
                    if s >= 1:
                        t = s - 1
                        pool.wait_ge(ln_n, NT * i + t + 1)
                        if t == 0:
                            pool.wait_ge(gb_ld, 32 * (i + 1))
                        pool.tensor_tensor(x[:, t, :], x[:, t, :], gb[:, 0, :], ALU.mult).then_inc(ln_g, 1)

            load_gb(0)
            for n in range(4, 8):
                gate_bias(n)
            norm_share(0)
            load_gb(1)
            gate_bias(8)
            norm_share(1)
            load_gb(2)
            pool.memset(ub[:], 0.0).then_inc(up_z, 1)
            for g in range(4):
                if g >= 2:
                    pool.wait_ge(pl_f, 2 * (g - 1))
                pool.dma_start(ic[:, g % 2, :], A["t_icnt"][g].partition_broadcast(P)).then_inc(ic_ld[g % 2], 16)
            for n in range(9, 16):
                gate_bias(n)
            norm_share(2)
            load_gb(3)
            norm_share(3)
            pool.wait_ge(fin2, 16 * 5)

        @block.tensor
        def _(pe):
            HP, UP_, WP = (hhi, hlo), (uhi, ulo), (whi, wlo)

            def weights_still(outs, w_of, a_of, nk):
                for k in range(nk):
                    for still, part in ((0, 0), (0, 1), (1, 0)):
                        for hf in range(2):
                            mm = pe.matmul(outs[hf], w_of(still, k), a_of(part, k, hf),
                                           start=(k == 0 and part == 0 and still == 0),
                                           stop=(k == nk - 1 and still == 1))
                return mm

            def tokens_still(out, a_of, w_of, nk):
                for k in range(nk):
                    for still, part in ((0, 0), (0, 1), (1, 0)):
                        mm = pe.matmul(out, a_of(still, k), w_of(part, k),
                                       start=(k == 0 and part == 0 and still == 0),
                                       stop=(k == nk - 1 and still == 1))
                return mm

            def w_cols(w, row, lo, n):
                return lambda part, k: WP[part][:, w % 2, k * row + lo:k * row + lo + n]

            def h_cols(buf, k0=0):
                return lambda part, k, hf: buf[part][:, k0 + k, hf * HALF:(hf + 1) * HALF]

            def h_tile(buf, t, k0=0):
                return lambda part, k: buf[part][:, k0 + k, t * P:(t + 1) * P]

            def mod_product(m):
                b = 4 + m % 2 if m < M_MIX else 7
                raw_ready(pe, mod_k[m])
                if m < M_MIX and m >= 2:
                    pe.wait_ge(mod_row, m - 1)
                if m >= M_MIX:
                    pe.wait_ge(mod_out, m)
                for k in range(KT):
                    g = k % 4
                    mm = pe.matmul(ps[32 * g:32 * g + 32, b * 512:b * 512 + BW], cpad[:, k, :],
                                   raw[:, mod_k[m] % 2, k * BW:(k + 1) * BW], start=(k < 4), stop=(k >= 4))
                mm.then_inc(mod_main, 1)

            def mod_turn(m):
                b = 6 + m % 2 if m < M_MIX else 7
                pe.wait_ge(mod_row, m + 1)
                if m < M_MIX and m >= 2:
                    pe.wait_ge(mod_out, m - 1)
                if m in gate_blocks:
                    for c in range(2):
                        mm = pe.matmul(bank(b, c * BW, (c + 1) * BW), head[:, P * (c + 1):P * (c + 2)],
                                       modrow[:, m % 2, :], start=True, stop=True)
                else:
                    for n in range(2):
                        mm = pe.transpose(bank(b, n * P, (n + 1) * P), modrow[:, m % 2, n * P:(n + 1) * P], ident)
                mm.then_inc(mod_tr, 1)

            pe.wait_ge(ld_head, 16)
            pe.wait_ge(ld_vec, 16 * 7)
            pe.transpose(bank(6, 0, 72), vec_rows[0:72, 0, :], ident[0:72, 0:72])
            pe.transpose(bank(6, 128, 224), vec_rows[0:96, 1, :], ident[0:96, 0:96]).then_inc(vec_tr, 1)
            for t in range(NT):
                pe.wait_ge(x_ld[t], 16)
                if t >= 2:
                    pe.wait_ge(xT_ev, t - 1)
                for f in range(KT):
                    mm = pe.transpose(bank(2 * (t % 2), f * P, (f + 1) * P), x[:, t, f * P:(f + 1) * P], ident)
                mm.then_inc(xT_tr, 1)
            pe.wait_ge(c_ok, 1)
            pe.wait_ge(vec_cp, 1)
            for m in range(M_MIX):
                mod_product(m)
                if m >= 1:
                    mod_turn(m - 1)
            mod_turn(M_MIX - 1)

            for jb in range(4):
                pe.wait_ge(lo_done, jb + 1)
                for m in range(2):
                    f = 2 * jb + m
                    if f == 0:
                        pe.wait_ge(h_lo, KT)
                    if f >= 2:
                        pe.wait_ge(xb_ev, f - 1)
                    b = 2 * (f % 2)
                    weights_still((bank(b, 0, HALF), bank(b + 1, 0, HALF)), w_cols(jb, BW, m * P, P), h_cols(HP), KT) \
                        .then_inc(xb_mm, 1)
            pe.wait_ge(dt_wl, 1)
            pe.wait_ge(mod_row, M_MIX)
            weights_still((ps[0:16, 4 * 512:4 * 512 + HALF], ps[0:16, 5 * 512:5 * 512 + HALF]),
                          lambda part, k: (wdth, wdtl)[part][:, k, :], h_cols(HP), KT).then_inc(dt_mm, 1)

            def turn_qk(n):
                pe.wait_ge(qk_rd, n + 1)
                if n >= 2:
                    pe.wait_ge(qk_ev, n - 1)
                else:
                    pe.wait_ge(xb_ev, KT)
                for hp in range(2):
                    mm = pe.transpose(bank(n % 2, hp * P, (hp + 1) * P), qk[:, n % 2, hp * P:(hp + 1) * P], ident)
                mm.then_inc(qk_tr, 1)

            for ib in range(8):
                pe.wait_ge(lo_done, 5 + ib)
                for t in range(NT):
                    g = 5 * ib + t
                    if g == 0:
                        pe.wait_ge(dt_x, 1)
                        pe.wait_ge(mod_out, M_MIX)
                    if g >= 4:
                        pe.wait_ge(ib_ev, g - 3)
                    tokens_still(bank(4 + g % 4, 0, BW), h_tile(HP, t), w_cols(4 + ib, BW, 0, BW), KT).then_inc(ib_mm, 1)
                    if g >= 21:
                        turn_qk(g - 21)
            turn_qk(19)

            pe.wait_ge(cv_ok, KT)
            for t in range(NT):
                if t < 2:
                    pe.wait_ge(qk_ev, 20)
                else:
                    pe.wait_ge(xt_ev, t - 1)
                for f in range(6):
                    mm = pe.transpose(bank(2 * (t % 2), f * P, (f + 1) * P), convT[:, f, t * P:(t + 1) * P], ident)
                mm.then_inc(xt_tr, 1)
            pe.wait_ge(dt_ok, 1)
            pe.wait_ge(ib_ev, 40)
            for t in range(NT):
                pe.transpose(bank(6, t * 16, t * 16 + 16), dtT[:, t * P:(t + 1) * P], ident[0:16, 0:16])
                mm = pe.transpose(bank(6, 80 + t * 16, 96 + t * 16), daT[:, t * P:(t + 1) * P], ident[0:16, 0:16])
            mm.then_inc(dtr, 1)
            pe.wait_ge(ld_mix, 16 * 16)
            for tt in range(2):
                for n in range(2):
                    for hp in range(2):
                        mm = pe.transpose(bank(4 + tt, (2 * n + hp) * P, (2 * n + hp + 1) * P),
                                          kc[:, tt, n, 2 * hp:2 * hp + 2, :].rearrange("p h d -> p (h d)"), ident)
            mm.then_inc(kc_tr, 1)
            pe.wait_ge(dtk, 1)
            for d in range(2):
                mm = pe.matmul(bank(7, 40 * d, 40 * d + 40), ssdc[:, d, :], datok[:, :, d, :], start=True, stop=True)
            mm.then_inc(acs_mm, 1)
            pe.wait_ge(xt_ev, NT)
            for d in range(2):
                for r in range(4):
                    mm = pe.transpose(bank(d, r * P, (r + 1) * P), sld[:, d, r, :], ident)
            mm.then_inc(sld_tr, 1)

            todo = [M_MIX, M_MIX]

            def site_product():
                if todo[0] < M_MIX + SITES:
                    mod_product(todo[0])
                    todo[0] += 1

            def site_turn():
                if todo[1] < todo[0]:
                    mod_turn(todo[1])
                    todo[1] += 1

            def chunk_r(n, c):
                if n == 0:
                    pe.wait_ge(hst_ok, 1)
                    pe.wait_ge(kc_ev, 1)
                else:
                    pe.wait_ge(seg_ok, 2 * n)
                for d in range(2):
                    for h in range(NH_B):
                        mm = pe.matmul(bank(2 * d, h * P, (h + 1) * P),
                                       datok[:, c, d, h:h + 1].to_broadcast([P, P]), ssdc[:, d, :],
                                       start=True, stop=True)
                    mm.then_inc(r_mm, 1)
                if n >= 1:
                    pe.wait_ge(m_ok, n)
                for g in range(2):
                    mm = pe.matmul(bank(4, g * P, (g + 1) * P), convT[:, 4 + g, c * P:(c + 1) * P],
                                   convT[:, 6 + g, c * P:(c + 1) * P], start=True, stop=True)
                mm.then_inc(g_mm, 1)

            def chunk_y(n, c):
                pe.wait_ge(m_ok, n + 1)
                if n >= 1:
                    pe.wait_ge(y_ok, n)
                for h in range(NH_B):
                    mm = pe.matmul(bank(5, h * DH, (h + 1) * DH), ef[:, h, :], xb[:, c, h * DH:(h + 1) * DH],
                                   start=True, stop=True)
                mm.then_inc(yd_mm, 1)

            pe.wait_ge(acs_ok, 1)
            chunk_r(0, ORDER[0])
            for n in range(NT):
                site_product()
                if n + 1 < NT:
                    chunk_r(n + 1, ORDER[n + 1])
                site_turn()
                chunk_y(n, ORDER[n])

            def add_to_state(s, d, c):
                pe.wait_ge(w_ok, s + 1)
                for g in range(2):
                    mm = pe.matmul(bank(2 + d, g * 256, (g + 1) * 256), xb[:, c, 512 + g * P:512 + (g + 1) * P],
                                   wst[:, s % 2, g * 256:(g + 1) * 256], start=True, stop=True)
                mm.then_inc(st_mm, 1)

            pe.wait_ge(seg_ok, 2 * NT)
            for i in range(4):
                for d in range(2):
                    c = i if d == 0 else 3 - i
                    if i > 0:
                        pe.wait_ge(h_ok, 2 * (i - 1) + d + 1)
                    for g in range(2):
                        mm = pe.matmul(bank(d, g * 256, (g + 1) * 256), convT[:, 6 + g, c * P:(c + 1) * P],
                                       hst[:, d, g * 256:(g + 1) * 256], start=True, stop=True)
                    mm.then_inc(off_mm, 1)
                    if i < 3:
                        add_to_state(2 * i + d, d, c)
                    if d == 0:
                        site_product()
                    else:
                        site_turn()
            for d in range(2):
                pe.wait_ge(h_ok, 5 + d)
                add_to_state(6 + d, d, 4)
            for d in range(2):
                pe.wait_ge(h_ok, 7 + d)
                pe.wait_ge(off_ok, 8)
                for r in range(4):
                    mm = pe.transpose(bank(d, r * P, (r + 1) * P), hst[:, d, r * P:(r + 1) * P], ident)
                mm.then_inc(nst_tr, 1)

            def scores(a):
                t, h = a // NH_A, a % NH_A
                hp, rows = h // 2, (DH * (h % 2), DH * (1 - h % 2))
                if a >= 1:
                    pe.wait_ge(ex_ok, a)
                else:
                    pe.wait_ge(nst_ev, 2)
                for part in range(2 if t < LAT else 1):
                    for n, r in enumerate(rows):
                        keys = (kT[r:r + DH, 2 * n + hp, part * 384:(part + 1) * 384] if t < LAT
                                else kTp[r:r + DH, 2 * n + hp, :])
                        mm = pe.matmul(bank(2 * n + part, 0, keys.shape[-1]),
                                       qT[r:r + DH, 2 * n + hp, t * P:(t + 1) * P], keys, start=True, stop=True)
                mm.then_inc(s_mm, 1)

            def turn_p(a):
                pe.wait_ge(p_ok, a + 1)
                if a >= 1:
                    pe.wait_ge(pt_ev, a)
                for n in range(6 if a // NH_A < LAT else 1):
                    mm = pe.transpose(bank(4, n * P, (n + 1) * P), e[:, a % 2, 0, n * P:(n + 1) * P], ident)
                mm.then_inc(pt_tr, 1)

            def pv(a):
                t, h = a // NH_A, a % NH_A
                pe.wait_ge(pt_ev, a + 1)
                if h == 0 and t >= 1:
                    pe.wait_ge(o_ok, t)
                nk = 6 if t < LAT else 1
                for n in range(nk):
                    mm = pe.matmul(bank(6, h * P, (h + 1) * P), pt[:, a % 2, n, :],
                                   v[:, n if t < LAT else 6, h * P:(h + 1) * P], start=(n == 0), stop=(n == nk - 1))
                mm.then_inc(pv_mm, 1)

            pe.wait_ge(y_ok, NT)
            for a in range(NA + 2):
                if a < NA:
                    scores(a)
                site_product()
                if 1 <= a <= NA:
                    turn_p(a - 1)
                site_turn()
                if a >= 2:
                    pv(a - 2)
            pe.wait_ge(yg_ok, NT)
            for m in range(M_MIX + SITES, M_MIX + SITES + 4):
                mod_product(m)
                mod_turn(m)

            for t in range(NT):
                pe.wait_ge(o_ok, t + 1)
                pe.wait_ge(yn_ok, t + 1)
                if t >= 2:
                    pe.wait_ge(mix_lo, t - 1)
                for f in range(4):
                    pe.transpose(bank(2 * (t % 2), f * P, (f + 1) * P), oa[:, t, f * P:(f + 1) * P], ident)
                for f in range(4):
                    mm = pe.transpose(bank(2 * (t % 2) + 1, f * P, (f + 1) * P), y[:, t, f * P:(f + 1) * P], ident)
                mm.then_inc(mix_tr, 1)

            def project_out(layer, ready, all_at_once):
                pe.wait_ge(mod_out, M_MIX + SITES + 4 if layer == 0 else 48)
                for ob in range(4):
                    w = W_OUT[layer] + ob
                    pe.wait_ge(lo_done, w + 1)
                    for t in range(NT):
                        g = 5 * ob + t
                        if ob == 0:
                            pe.wait_ge(ready, KT if all_at_once else t + 1)
                        if g >= 4:
                            pe.wait_ge(out_ev[layer], g - 3)
                        tokens_still(bank(4 + g % 4, 0, BW), h_tile(HP, t), w_cols(w, BW, 0, BW), KT) \
                            .then_inc(out_mm[layer], 1)

            def norm_turn(i):
                for t in range(NT):
                    pe.wait_ge(ln_x, NT * i + t + 1)
                    if t >= 2:
                        pe.wait_ge(ln_lo, NT * i + t - 1)
                    for f in range(KT):
                        mm = pe.transpose(bank(2 * (t % 2), f * P, (f + 1) * P), x[:, t, f * P:(f + 1) * P], ident)
                    mm.then_inc(ln_tr, 1)

            def up(layer, u, i=None):
                w = w_ord[S.index(("up", layer, u))]
                pe.wait_ge(lo_done, lin(w + 1, 8, i))
                for m in range(2):
                    n = 2 * u + m
                    if n == 0:
                        pe.wait_ge(ln_lo, NT * (2 * layer + 1))
                    if n >= 2:
                        pe.wait_ge(relu_ok[layer], lin(n - 1, 8, i))
                    b = 2 * (n % 2)
                    weights_still((bank(b, 0, HALF), bank(b + 1, 0, HALF)), w_cols(w, BW, m * P, P), h_cols(HP), KT) \
                        .then_inc(up_mm[layer], 1)

            def down(layer, d, i=None):
                w = w_ord[S.index(("down", layer, d))]
                c = d // 2
                pe.wait_ge(lo_done, lin(w + 1, 8, i))
                pe.wait_ge(sq_lo[layer], lin(4 * (c + 1), 8, i))
                for t in range(NT):
                    g = 5 * d + t
                    if g >= 4:
                        pe.wait_ge(acc_ok[layer], lin(g - 3, 20, i))
                    tokens_still(bank(4 + g % 4), h_tile(UP_, t, 4 * (c % 2)), w_cols(w, 512, 0, 512), 4) \
                        .then_inc(dn_mm[layer], 1)

            def mlp(layer):
                for kind, n, i in mlp_steps(pe):
                    (up if kind == "up" else down)(layer, n, i)

            project_out(0, mix_lo, False)
            norm_turn(0)
            mlp(0)
            norm_turn(1)

            for jb in range(4):
                w = W_IN1 + jb
                pe.wait_ge(lo_done, w + 1)
                for m in range(2):
                    f = 2 * jb + m
                    if f == 0:
                        pe.wait_ge(ln_lo, 2 * NT)
                    if f >= 2:
                        pe.wait_ge(u_ev, f - 1)
                    b = 2 * (f % 2)
                    weights_still((bank(b, 0, HALF), bank(b + 1, 0, HALF)), w_cols(w, BW, m * P, P), h_cols(HP), KT) \
                        .then_inc(u_mm, 1)
            w = W_IN1 + 4
            pe.wait_ge(lo_done, w + 1)
            for f in range(KT):
                g, m = f // 2, f % 2
                pe.wait_ge(pl_lo, 2 * g + 2)
                if f < 2:
                    pe.wait_ge(u_ev, KT)
                else:
                    pe.wait_ge(px_f, f - 1)
                b = 2 * (f % 2)
                weights_still((bank(b, 0, HALF), bank(b + 1, 0, HALF)), w_cols(w, BW, 2 * g * BW + m * P, P),
                              h_cols(UP_, 2 * g), 2).then_inc(px_mm, 1)
            pe.wait_ge(acc_ok[0], 80)
            for m in range(M_MIX + SITES + 4, 48):
                mod_product(m)
                mod_turn(m)
            project_out(1, px_lo, True)
            norm_turn(2)
            mlp(1)

        @block.scalar
        def _(act):
            def split_hi(w, i=None):
                k = w_k[w]
                raw_ready(act, k, i)
                if w >= 2:
                    s_, val, per = read_by_pe(w - 2)
                    act.wait_ge(s_, lin(val, per, i))
                act.activation(whi[:, w % 2, :], raw[:, k % 2, :], ACT.Copy).then_inc(hi_done, 1)

            def mod_rows(m):
                b = 4 + m % 2 if m < M_MIX else 7
                act.wait_ge(mod_main, m + 1)
                if m >= 2:
                    act.wait_ge(mod_tr, m - 1)
                act.activation(modrow[:, m % 2, :], bank(b, 0, BW), ACT.Copy).then_inc(mod_row, 1)

            def six(b, cols):
                return ps[:, b * 512:b * 512 + cols]

            for t in range(NT):
                src = x_sample[0, t * P:(t + 1) * P, :] if t < LAT else x_prompt[0]
                act.dma_start(x[:, t, :], src).then_inc(x_ld[t], 16)
            act.wait_ge(vec_cp, 1)
            act.activation(thc[:, 0, :], vecT[:, 0:16], ACT.Tanh, scale=0.5).then_inc(c_th, 1)
            act.wait_ge(lam_s, 2)
            act.activation(lexp, lsum, ACT.Exp).then_inc(lam_e, 1)
            for t in range(NT):
                act.wait_ge(xT_tr, t + 1)
                act.activation(xT[:, :, t * P:(t + 1) * P],
                               six(2 * (t % 2), D).rearrange("p (f n) -> p f n", f=KT), ACT.Copy).then_inc(xT_ev, 1)
            for m in range(M_MIX):
                mod_rows(m)
            for f in range(KT):
                act.wait_ge(h_md, f + 1)
                act.activation(hhi[:, f, :], xT[:, f, :], ACT.Copy).then_inc(h_hi, 1)
            act.wait_ge(ld_small, 16 * 6)
            act.activation(wdth[:], wdt[:], ACT.Copy).then_inc(dt_w, 1)
            act.activation(db[:, 2:3], db[:, 1:2], ACT.Exp).then_inc(dt_w, 1)
            split_hi(0)

            def conv_tanh(f):
                act.wait_ge(cv_v, f + 1)
                if f >= 2:
                    act.wait_ge(cv_ok, f - 1)
                act.activation(tmp[:, f % 2, 0:TOK], convT[:, f, :], ACT.Tanh).then_inc(cv_th, 1)

            for jb in range(4):
                split_hi(jb + 1)
                for m in range(2):
                    f = 2 * jb + m
                    act.wait_ge(xb_mm, f + 1)
                    if f == 0:
                        act.wait_ge(cpz, 1)
                    if f >= 2:
                        act.wait_ge(cv_v, f - 1)
                    b = 2 * (f % 2)
                    act.activation(craw[:, f % 2, 2:2 + HALF], bank(b, 0, HALF), ACT.Copy)
                    act.activation(craw[:, f % 2, 2 + HALF:514], bank(b + 1, 0, 512 - HALF), ACT.Copy)
                    act.activation(craw[:, f % 2, 518:646], bank(b + 1, 512 - HALF, HALF), ACT.Copy).then_inc(xb_ev, 1)
                    if f >= 1:
                        conv_tanh(f - 1)
            conv_tanh(KT - 1)
            act.wait_ge(dt_x, 2)
            act.activation(dtb[:], dta[:], ACT.Exp, scale=-1.0).then_inc(dt_e, 1)
            act.wait_ge(dt_u, 1)
            act.activation(dtc[:], dta[:], ACT.Ln).then_inc(dt_l, 1)

            def evac_qk(n):
                blk, t = n // NT, n % NT
                act.wait_ge(qk_tr, n + 1)
                dst = (qT[:, 2 * blk:2 * blk + 2, t * P:(t + 1) * P] if blk < 2 else
                       kT[:, 2 * blk - 4:2 * blk - 2, PAST + t * P:PAST + (t + 1) * P] if t < LAT else
                       kTp[:, 2 * blk - 4:2 * blk - 2, :])
                act.activation(dst, bank(n % 2, 0, 256).rearrange("p (h n) -> p h n", h=2), ACT.Copy).then_inc(qk_ev, 1)

            for ib in range(8):
                if ib < 7:
                    split_hi(5 + ib)
                for t in range(NT):
                    g = 5 * ib + t
                    if ib in (2, 3):
                        act.wait_ge(ib_mm, g + 1)
                        if g == 10:
                            act.wait_ge(cv_ok, KT)
                        if g >= 12:
                            act.wait_ge(ib_ev, g - 1)
                        act.activation(zth[:, g % 2, :], bank(4 + g % 4, 0, BW), ACT.Tanh, scale=0.5).then_inc(ib_z, 1)
                    if g >= 21:
                        evac_qk(g - 21)
            evac_qk(19)
            for t in range(NT):
                act.wait_ge(xt_tr, t + 1)
                act.activation(xb[:, t, :], six(2 * (t % 2), 768), ACT.Copy).then_inc(xt_ev, 1)
            act.wait_ge(sld_tr, 1)
            act.activation(hst[:].rearrange("p d n -> p (d n)"), six(0, 1024), ACT.Copy).then_inc(hst_ok, 1)

            todo = [M_MIX]

            def site_rows():
                if todo[0] < M_MIX + SITES:
                    mod_rows(todo[0])
                    todo[0] += 1

            for n in range(NT):
                for d, buf in enumerate((ef, eb)):
                    act.wait_ge(seg_ok, 2 * n + d + 1)
                    act.activation(buf[:], buf[:], ACT.Exp).then_inc(eexp, 1)
                site_rows()
            act.wait_ge(dec_s, 1)
            act.activation(dtw, dtw, ACT.Exp).then_inc(dec_e, 1)
            act.activation(cdec, rend, ACT.Exp).then_inc(dec_e, 1)
            act.activation(eacs, acs, ACT.Exp).then_inc(dec_e, 1)
            for i in range(4):
                site_rows()
            for d in range(2):
                act.wait_ge(nst_tr, d + 1)
                act.activation(sso[:, d].rearrange("p r n -> p (r n)"), bank(d), ACT.Copy).then_inc(nst_ev, 1)
            for t in range(NT):
                act.wait_ge(yg_ok, t + 1)
                if t >= 1:
                    act.wait_ge(yg_sq, t)
                if t >= 2:
                    act.wait_ge(yg_rs, t - 1)
                act.activation(osq[:], y[:, t, :], ACT.Square, accum_out=ysq[:, t % 2:t % 2 + 1]).then_inc(yg_sq, 1)

            def exps(a):
                w_ = KEYS if a // NH_A < LAT else P
                act.wait_ge(mx_ok, a + 1)
                if a >= 2:
                    act.wait_ge(pt_tr, a - 1)
                for n in range(2):
                    src = two(2 * n, 384) if w_ == KEYS else bank(2 * n, 0, P)
                    dst = (e[:, a % 2, n, :].rearrange("p (b n) -> p b n", b=2) if w_ == KEYS
                           else e[:, a % 2, n, 0:P])
                    ins = act.activation(dst, src, ACT.Exp, bias=nmx[:, a % 2, n:n + 1], scale=SCALE,
                                         accum_out=esum[:, a % 2, n:n + 1])
                ins.then_inc(ex_ok, 1)

            def evac_p(a):
                act.wait_ge(pt_tr, a + 1)
                if a >= 2:
                    act.wait_ge(pv_mm, a - 1)
                n = 6 if a // NH_A < LAT else 1
                act.activation(pt[:, a % 2, 0:n, :].rearrange("p k n -> p (k n)"), six(4, n * P), ACT.Copy) \
                    .then_inc(pt_ev, 1)

            for a in range(NA + 3):
                if a < NA:
                    exps(a)
                if 1 <= a <= NA:
                    evac_p(a - 1)
                if a < NA + 2:
                    site_rows()
                if a >= 3 and (a - 3) % NH_A == NH_A - 1:
                    t = (a - 3) // NH_A
                    act.wait_ge(pv_mm, NH_A * (t + 1))
                    if t >= 1:
                        act.wait_ge(o_sq, t)
                    if t >= 2:
                        act.wait_ge(o_rs, t - 1)
                    for h in range(NH_A):
                        ins = act.activation(osq[:, h * P:(h + 1) * P], bank(6, h * P, (h + 1) * P), ACT.Square,
                                             accum_out=ss[:, t % 2, h:h + 1])
                    ins.then_inc(o_sq, 1)
            for m in range(M_MIX + SITES, M_MIX + SITES + 4):
                mod_rows(m)
            for t in range(NT):
                act.wait_ge(mix_tr, t + 1)
                act.activation(hhi[:, :, t * P:(t + 1) * P], six(2 * (t % 2), D).rearrange("p (f n) -> p f n", f=KT),
                               ACT.Copy).then_inc(mix_hi, 1)

            def norm_high(i):
                layer, q = i // 2, 2
                if i % 2 == 1:
                    layer, q = layer + 1, 0
                for t in range(NT):
                    c = int(t == LAT)
                    act.wait_ge(ln_tr, NT * i + t + 1)
                    if t >= 2:
                        act.wait_ge(ln_lo, NT * i + t - 1)
                    for f in range(4):
                        act.activation(tmp[:, t % 2, f * P:(f + 1) * P], bank(2 * (t % 2), f * P, (f + 1) * P),
                                       ACT.Identity, bias=modT[:, layer, q, f, c:c + 1],
                                       scale=modT[:, layer, q + 1, f, c:c + 1]).then_inc(ln_ma, 1)
                    act.wait_ge(ln_ma, 4 * (NT * i + t) + 4)
                    act.wait_ge(ln_md, NT * i + t + 1)
                    act.activation(hhi[:, :, t * P:(t + 1) * P], tmp[:, t % 2, :].rearrange("p (f n) -> p f n", f=KT),
                                   ACT.Copy).then_inc(ln_hi, 1)

            def relu_square(layer, u, i=None):
                for m in range(2):
                    n = 2 * u + m
                    c = u // 2
                    act.wait_ge(up_mm[layer], lin(n + 1, 8, i))
                    if n >= 2:
                        act.wait_ge(sq_lo[layer], lin(n - 1, 8, i))
                    b = 2 * (n % 2)
                    r = tmp[:, n % 2, 0:TOK]
                    act.activation(r.rearrange("p (b n) -> p b n", b=2), two(b), ACT.Relu).then_inc(relu_ok[layer], 1)
                    act.wait_ge(relu_ok[layer], lin(n + 1, 8, i))
                    if c >= 2:
                        act.wait_ge(dn_mm[layer], lin(10 * (c - 1), 20, i))
                    act.activation(uhi[:, 4 * (c % 2) + n % 4, :], r, ACT.Square).then_inc(sq_hi[layer], 1)

            def mlp(layer):
                for kind, n, i in mlp_steps(act):
                    w = w_ord[S.index((kind, layer, n))]
                    if w + 1 < len(w_k):
                        split_hi(w + 1, i)
                    if kind == "up":
                        relu_square(layer, n, i)

            def pool_high(f):
                act.wait_ge(pl_f, f + 1)
                w2 = POOL_W[f // 2] // 2
                pos, t0, cnt = SEG[0]
                act.activation(uhi[:, f, t0:t0 + cnt], pb[:, f % 3, pos - w2:pos - w2 + cnt], ACT.Copy)
                pos, t0, cnt = SEG[1]
                act.activation(uhi[:, f, t0:t0 + cnt], pb[:, f % 3, pos - w2:pos - w2 + cnt], ACT.Copy).then_inc(pl_hi, 1)

            split_hi(W_OUT[0])
            for ob in range(4):
                split_hi(W_OUT[0] + ob + 1)
            norm_high(0)
            mlp(0)
            norm_high(1)
            for jb in range(4):
                split_hi(W_IN1 + jb + 1)
                for m in range(2):
                    f = 2 * jb + m
                    act.wait_ge(u_mm, f + 1)
                    if f == 0:
                        act.wait_ge(up_z, 1)
                    if f >= 2:
                        act.wait_ge(pl_f, f - 1)
                    b = 2 * (f % 2)
                    act.activation(ub[:, f % 2, 8:8 + HALF], bank(b, 0, HALF), ACT.Copy)
                    act.activation(ub[:, f % 2, 8 + HALF:520], bank(b + 1, 0, 512 - HALF), ACT.Copy)
                    act.activation(ub[:, f % 2, 536:664], bank(b + 1, 512 - HALF, HALF), ACT.Copy).then_inc(u_ev, 1)
                    if f >= 1:
                        pool_high(f - 1)
            pool_high(KT - 1)
            for f in range(KT):
                act.wait_ge(px_mm, f + 1)
                if f >= 2:
                    act.wait_ge(px_lo, f - 1)
                r = tmp[:, f % 2, 0:TOK]
                act.activation(r.rearrange("p (b n) -> p b n", b=2), two(2 * (f % 2)), ACT.Copy,
                               scale=vecT[:, 64 + f:65 + f]).then_inc(px_f, 1)
                act.wait_ge(px_f, f + 1)
                act.activation(hhi[:, f, :], r, ACT.Copy).then_inc(px_hi, 1)
            for m in range(M_MIX + SITES + 4, 48):
                mod_rows(m)
            split_hi(W_OUT[1])
            for ob in range(4):
                split_hi(W_OUT[1] + ob + 1)
            norm_high(2)
            mlp(1)

        @block.vector
        def _(dve):
            vn = [0]

            def mark(ins):
                ins.then_inc(vs, 1)
                vn[0] += 1

            def settle():
                dve.wait_ge(vs, vn[0])

            def split_lo(w, i=None):
                dve.wait_ge(hi_done, lin(w + 1, 8, i))
                dve.tensor_tensor(wlo[:, w % 2, :], raw[:, w_k[w] % 2, :], whi[:, w % 2, :].bitcast(F32),
                                  ALU.subtract).then_inc(lo_done, 1)

            def mod_finish(m):
                _, layer, b = S[mod_k[m]]
                j, q = b // 4, b % 4
                bk = 6 + m % 2 if m < M_MIX else 7
                dve.wait_ge(mod_tr, m + 1)
                if m in gate_blocks:
                    dve.wait_ge(gbias_ld, 16 * (gate_blocks.index(m) + 1))
                    dve.tensor_tensor(gate[:, j // 3, :, q * BW:(q + 1) * BW],
                                      bank(bk).rearrange("p (c n) -> p c n", c=2),
                                      gbias[:].unsqueeze(1).to_broadcast([P, 2, BW]), ALU.add).then_inc(mod_out, 1)
                    return
                if m >= 2:
                    dve.wait_ge(mod_out, m - 1)
                r = red[:, m % 2, :].rearrange("p (m c) -> p m c", m=2)
                src = bank(bk, 0, 256).rearrange("p (m g c) -> p m c g", m=2, g=4)[:, :, 0:2, :]
                mark(dve.tensor_reduce(r, src, AX.X, ALU.add))
                settle()
                for n in range(2):
                    ins = dve.tensor_scalar(modT[:, layer, 2 * (j // 3) + j % 3, 2 * q + n, :], r[:, n, :],
                                            bmodT[:, 48 * layer + 2 * b + n:48 * layer + 2 * b + n + 1],
                                            1.0 if j % 3 == 1 else 0.0, ALU.add, ALU.add)
                    if n == 0:
                        mark(ins)
                ins.then_inc(mod_out, 1)

            dve.wait_ge(vec_tr, 1)
            mark(dve.tensor_copy(vecT[:], bank(6, 0, 72)))
            dve.tensor_copy(bmodT[:], bank(6, 128, 224)).then_inc(vec_cp, 1)
            dve.wait_ge(ld_lam, 64)
            settle()
            for n in range(2):
                mark(dve.tensor_tensor(lamv[:, 2 * n, :], lamv[:, 2 * n, :], lamv[:, 2 * n + 1, :], ALU.mult))
            settle()
            for n in range(2):
                dve.reduce_sum(lsum[:, n:n + 1], lamv[:, 2 * n, :], AX.X).then_inc(lam_s, 1)
            dve.wait_ge(c_th, 1)
            dve.wait_ge(cz, 1)
            mark(dve.scalar_tensor_tensor(thc[:, 1, :], thc[:, 0, :], 1.0, vecT[:, 0:16], ALU.add, ALU.mult))
            settle()
            dve.tensor_scalar(cpad[:, :, 0:2], thc[:, 1, :].rearrange("p (c k) -> p k c", c=2), 0.5, None,
                              ALU.mult).then_inc(c_ok, 1)
            mark(dve.tensor_scalar(vecT[:, 16:64], vecT[:, 16:64], 0.5, None, ALU.mult))
            dve.wait_ge(lam_e, 1)
            mark(dve.tensor_tensor(nlam, lexp[:, 1:2], lexp[:, 0:1], ALU.subtract))
            settle()
            mark(dve.tensor_scalar(nlam, nlam, -LAM_INIT, None, ALU.add))
            for m in range(M_MIX):
                mod_finish(m)
            dve.wait_ge(mod_out, M_MIX)
            dve.wait_ge(xT_ev, NT)

            def low_of_h(f):
                dve.wait_ge(h_hi, f + 1)
                dve.tensor_tensor(hlo[:, f, :], xT[:, f, :], hhi[:, f, :].bitcast(F32), ALU.subtract).then_inc(h_lo, 1)

            for f in range(KT):
                for c, (lo, hi) in enumerate(((0, 512), (512, TOK))):
                    ins = dve.tensor_scalar(xT[:, f, lo:hi], xT[:, f, lo:hi], modT[:, 0, 1, f, c:c + 1],
                                            modT[:, 0, 0, f, c:c + 1], ALU.mult, ALU.add)
                ins.then_inc(h_md, 1)
                if f >= 1:
                    low_of_h(f - 1)
            low_of_h(KT - 1)
            split_lo(0)
            dve.wait_ge(dt_w, 2)
            dve.tensor_tensor(wdtl[:], wdt[:], wdth[:].bitcast(F32), ALU.subtract).then_inc(dt_wl, 1)

            def conv(f):
                dve.wait_ge(xb_ev, f + 1)
                for j in range(5):
                    for n, (pos, t0, cnt) in enumerate(CSEG):
                        src = craw[:, f % 2, pos - 2 + j:pos - 2 + j + cnt]
                        dst = convT[:, f, t0:t0 + cnt]
                        tap = vecT[:, 16 + 8 * j + f:17 + 8 * j + f]
                        if j == 0:
                            ins = dve.tensor_scalar(dst, src, tap, vecT[:, 56 + f:57 + f], ALU.mult, ALU.add)
                        else:
                            ins = dve.scalar_tensor_tensor(dst, src, tap, dst, ALU.mult, ALU.add)
                        if j < 4 or n == 0:
                            mark(ins)
                    if j < 4:
                        settle()
                ins.then_inc(cv_v, 1)

            def conv_silu(f):
                dve.wait_ge(cv_th, f + 1)
                dve.scalar_tensor_tensor(convT[:, f, :], tmp[:, f % 2, 0:TOK], 1.0, convT[:, f, :],
                                         ALU.add, ALU.mult).then_inc(cv_ok, 1)

            for jb in range(4):
                split_lo(jb + 1)
                for m in range(2):
                    f = 2 * jb + m
                    conv(f)
                    if f >= 1:
                        conv_silu(f - 1)
            conv_silu(KT - 1)

            dve.wait_ge(dt_mm, 1)
            dve.tensor_scalar(dtT[:].rearrange("p (b n) -> p b n", b=2),
                              ps[0:16, 4 * 512:6 * 512].rearrange("p (b n) -> p b n", b=2)[:, :, 0:HALF],
                              db[:, 0:1], None, ALU.add).then_inc(dt_x, 1)
            dve.wait_ge(dt_x, 1)
            mark(dve.tensor_scalar(dta[:], dtT[:], -1.0, None, ALU.mult))
            settle()
            dve.tensor_tensor(dta[:], dta[:], dtT[:], ALU.max).then_inc(dt_x, 1)
            dve.wait_ge(dt_e, 1)
            dve.tensor_scalar(dta[:], dtb[:], 1.0, None, ALU.add).then_inc(dt_u, 1)
            dve.wait_ge(dt_u, 1)
            mark(dve.reciprocal(dtd[:], dta[:]))
            dve.wait_ge(dt_l, 1)
            mark(dve.tensor_scalar(dta[:], dta[:], -1.0, None, ALU.add))
            settle()
            mark(dve.tensor_tensor(dta[:], dtb[:], dta[:], ALU.subtract))
            settle()
            mark(dve.tensor_tensor(dta[:], dta[:], dtd[:], ALU.mult))
            settle()
            mark(dve.tensor_tensor(dtc[:], dtc[:], dta[:], ALU.add))
            settle()
            mark(dve.scalar_tensor_tensor(dtT[:], dtT[:], 0.0, dtc[:], ALU.max, ALU.add))
            settle()
            dve.tensor_scalar(daT[:], dtT[:], db[:, 2:3], -1.0, ALU.mult, ALU.mult).then_inc(dt_ok, 1)

            def evac_in(ib, t):
                g = 5 * ib + t
                src = bank(4 + g % 4, 0, BW)
                dve.wait_ge(ib_mm, g + 1)
                if ib < 2:
                    dve.tensor_copy(v[:, 2 + t, ib * BW:(ib + 1) * BW], src).then_inc(ib_ev, 1)
                    return
                if ib < 4:
                    dve.wait_ge(ib_z, g - 9)
                    dve.scalar_tensor_tensor(zs[:, t, (ib - 2) * BW:(ib - 1) * BW], zth[:, g % 2, :], 1.0, src,
                                             ALU.add, ALU.mult).then_inc(ib_ev, 1)
                    return
                n, blk = g - 20, ib - 4
                if n >= 2:
                    dve.wait_ge(qk_tr, n - 1)
                flat = qk[:, n % 2, :]
                if t == LAT:
                    if blk >= 2:
                        mark(dve.tensor_copy(knew[:, blk - 2, :], src))
                    if blk % 2 == 0:
                        mark(dve.tensor_copy(flat, src))
                    else:
                        dst = flat.rearrange("p (g a d) -> p g a d", g=2, a=2)
                        s4 = src.rearrange("p (g a d) -> p g a d", g=2, a=2)
                        for a in range(2):
                            mark(dve.tensor_copy(dst[:, :, a, :], s4[:, :, 1 - a, :]))
                    settle()
                    dve.nop().then_inc(ib_ev, 1)
                    dve.nop().then_inc(qk_rd, 1)
                    return
                s8 = src.rearrange("p (m f) -> p m f", f=32)
                for k_, dst in ((0, ra), (1, rb)):
                    mark(dve.tensor_tensor(dst.rearrange("p (m f) -> p m f", f=32), s8,
                                           rp[:, t, k_, :].unsqueeze(1).to_broadcast([P, 8, 32]), ALU.mult))
                settle()
                a4 = ra.rearrange("p (h u f) -> p h u f", h=4, u=2)
                b4 = rb.rearrange("p (h u f) -> p h u f", h=4, u=2)
                o4 = flat.rearrange("p (h u f) -> p h u f", h=4, u=2)
                o4s = flat.rearrange("p (g a u f) -> p g a u f", g=2, a=2, u=2)
                for u, op in ((0, ALU.subtract), (1, ALU.add)):
                    if blk % 2 == 0:
                        mark(dve.tensor_tensor(o4[:, :, u, :], a4[:, :, u, :], b4[:, :, 1 - u, :], op))
                    else:
                        for a in range(2):
                            mark(dve.tensor_tensor(o4s[:, :, a, u, :], a4[:, 1 - a::2, u, :], b4[:, 1 - a::2, 1 - u, :], op))
                settle()
                dve.nop().then_inc(ib_ev, 1)
                dve.nop().then_inc(qk_rd, 1)

            dve.wait_ge(ld_small, 16 * 6)
            for ib in range(8):
                if ib < 7:
                    split_lo(5 + ib)
                for t in range(NT):
                    evac_in(ib, t)

            dve.wait_ge(dtr, 1)
            dve.tensor_copy(sm[:, 0:160], bank(6, 0, 160)).then_inc(dtk, 1)
            dve.wait_ge(kc_tr, 1)
            for tt in range(2):
                ins = dve.tensor_copy(kT[:, :, tt * P:(tt + 1) * P], bank(4 + tt).rearrange("p (m n) -> p m n", m=4))
                if tt == 0:
                    mark(ins)
            ins.then_inc(kc_ev, 1)
            dve.wait_ge(acs_mm, 1)
            dve.tensor_copy(sm[:, 160:240], bank(7, 0, 80)).then_inc(acs_ok, 1)
            dve.wait_ge(acs_ok, 1)
            mark(dve.tensor_scalar(subw[:], subw[:], 1.0 - LAM_INIT, None, ALU.mult))

            todo = [M_MIX]

            def site_finish():
                if todo[0] < M_MIX + SITES:
                    mod_finish(todo[0])
                    todo[0] += 1

            def per_head(ap, n):
                return ap.unsqueeze(2).to_broadcast([P, NH_B, n])

            def heads_of(ap):
                return ap.rearrange("p (h d) -> p h d", h=NH_B)

            for n in range(NT):
                c = ORDER[n]
                for d, buf in enumerate((ef, eb)):
                    dve.wait_ge(r_mm, 2 * n + d + 1)
                    if d == 0 and n >= 1:
                        dve.wait_ge(yd_mm, n)
                    rr_ = ps[:, 1024 * d:1024 * d + 1024].rearrange("p (h l) -> p h l", h=NH_B)
                    mark(dve.tensor_copy(rend[:, d, c, :], rr_[:, :, P - 1 if d == 0 else 0]))
                    for h in range(NH_B):
                        ins = dve.scalar_tensor_tensor(buf[:, h, :], rr_[:, h, :], acs[:, d, c, h:h + 1],
                                                       ssdc[:, 2 + d, :], ALU.subtract, ALU.add)
                        if h < NH_B - 1:
                            mark(ins)
                    ins.then_inc(seg_ok, 1)
                for d, buf in enumerate((ef, eb)):
                    dve.wait_ge(eexp, 2 * n + d + 1)
                    mark(dve.tensor_tensor(buf[:], buf[:], per_head(dtok[:, c, d, :], P), ALU.mult))
                settle()
                mark(dve.tensor_tensor(ef[:], ef[:], eb[:], ALU.add))
                settle()
                dve.wait_ge(g_mm, n + 1)
                ef4 = ef[:].rearrange("p (g q) l -> p g q l", g=2)
                dve.tensor_tensor(ef4, ef4, bank(4, 0, 256).rearrange("p (g l) -> p g l", g=2).unsqueeze(2)
                                  .to_broadcast([P, 2, 4, P]), ALU.mult).then_inc(m_ok, 1)
                mark(dve.tensor_tensor(heads_of(y[:, c, :]), heads_of(xb[:, c, 0:512]), per_head(dsk[:], DH), ALU.mult))
                dve.wait_ge(yd_mm, n + 1)
                settle()
                dve.tensor_tensor(y[:, c, :], y[:, c, :], bank(5), ALU.add).then_inc(y_ok, 1)
                site_finish()

            settle()
            dve.tensor_tensor(dtw, rend, acs, ALU.subtract).then_inc(dec_s, 1)
            dve.wait_ge(dec_e, 3)
            mark(dve.tensor_tensor(dtw, dtw, dtok.rearrange("p t d h -> p d t h"), ALU.mult))
            settle()

            def weighted(s, d, c):
                if s >= 2:
                    dve.wait_ge(st_mm, s - 1)
                dve.tensor_tensor(heads_of(wst[:, s % 2, :]), heads_of(xb[:, c, 0:512]), per_head(dtw[:, d, c, :], DH),
                                  ALU.mult).then_inc(w_ok, 1)

            dve.wait_ge(y_ok, NT)
            dve.wait_ge(hst_ok, 1)
            for i in range(4):
                for d in range(2):
                    if i < 3:
                        weighted(2 * i + d, d, i if d == 0 else 3 - i)
                for d in range(2):
                    c = i if d == 0 else 3 - i
                    dve.wait_ge(off_mm, 2 * i + d + 1)
                    mark(dve.tensor_tensor(heads_of(yt[:]), heads_of(bank(d)), per_head(eacs[:, d, c, :], DH), ALU.mult))
                    if i < 3:
                        mark(dve.tensor_tensor(heads_of(hst[:, d, :]), heads_of(hst[:, d, :]),
                                               per_head(cdec[:, d, c, :], DH), ALU.mult))
                    settle()
                    if i < 3:
                        dve.wait_ge(st_mm, 2 * i + d + 1)
                        dve.tensor_tensor(hst[:, d, :], hst[:, d, :], bank(2 + d), ALU.add).then_inc(h_ok, 1)
                    dve.tensor_tensor(y[:, c, :], y[:, c, :], yt[:], ALU.add).then_inc(off_ok, 1)
                    dve.wait_ge(off_ok, 2 * i + d + 1)
                site_finish()
            for d in range(2):
                weighted(6 + d, d, 4)
            for d in range(2):
                dve.wait_ge(st_mm, 7 + d)
                dve.tensor_copy(hst[:, d, :], bank(2 + d)).then_inc(h_ok, 1)
            dve.wait_ge(off_ok, 8)
            for t in range(NT):
                dve.scalar_tensor_tensor(y[:, t, :], y[:, t, :], 0.5, zs[:, t, :], ALU.mult, ALU.mult).then_inc(yg_ok, 1)
            for t in range(NT):
                dve.wait_ge(yg_rs, t + 1)
                dve.scalar_tensor_tensor(y[:, t, :], y[:, t, :], yrs[:, t % 2:t % 2 + 1], normw[:],
                                         ALU.mult, ALU.mult).then_inc(yn_ok, 1)

            def maxima(a):
                dve.wait_ge(s_mm, a + 1)
                if a >= 2:
                    dve.wait_ge(ex_ok, a - 1)
                for n in range(2):
                    if a // NH_A < LAT:
                        mark(dve.tensor_reduce(mx[:, a % 2, n:n + 1], two(2 * n, 384), AX.XY, ALU.max))
                    else:
                        mark(dve.tensor_reduce(mx[:, a % 2, n:n + 1], bank(2 * n, 0, P), AX.X, ALU.max))
                settle()
                dve.tensor_scalar(nmx[:, a % 2, :], mx[:, a % 2, :], -SCALE, None, ALU.mult).then_inc(mx_ok, 1)

            def differ(a):
                w_ = KEYS if a // NH_A < LAT else P
                dve.wait_ge(ex_ok, a + 1)
                mark(dve.reciprocal(rec[:, a % 2, :], esum[:, a % 2, :]))
                settle()
                mark(dve.tensor_tensor(rec[:, a % 2, 1:2], rec[:, a % 2, 1:2], nlam, ALU.mult))
                e1, e2 = e[:, a % 2, 0, 0:w_], e[:, a % 2, 1, 0:w_]
                mark(dve.tensor_scalar(e1, e1, rec[:, a % 2, 0:1], None, ALU.mult))
                settle()
                dve.scalar_tensor_tensor(e1, e2, rec[:, a % 2, 1:2], e1, ALU.mult, ALU.add).then_inc(p_ok, 1)

            for a in range(NA + 3):
                if a < NA:
                    maxima(a)
                if 1 <= a <= NA:
                    differ(a - 1)
                if a < NA + 2:
                    site_finish()
                if a >= 3 and (a - 3) % NH_A == NH_A - 1:
                    t = (a - 3) // NH_A
                    dve.wait_ge(o_rs, t + 1)
                    for h in range(NH_A):
                        ins = dve.scalar_tensor_tensor(oa[:, t, h * P:(h + 1) * P], bank(6, h * P, (h + 1) * P),
                                                       rr[:, t % 2, h:h + 1], subw[:], ALU.mult, ALU.mult)
                        if h < NH_A - 1:
                            mark(ins)
                    ins.then_inc(o_ok, 1)
            for m in range(M_MIX + SITES, M_MIX + SITES + 4):
                mod_finish(m)
            for t in range(NT):
                dve.wait_ge(mix_hi, t + 1)
                dve.tensor_tensor(hlo[:, :, t * P:(t + 1) * P],
                                  ps[:, 1024 * (t % 2):1024 * (t % 2) + D].rearrange("p (f n) -> p f n", f=KT),
                                  hhi[:, :, t * P:(t + 1) * P].bitcast(F32), ALU.subtract).then_inc(mix_lo, 1)

            def residual(i, t, cols):
                dve.scalar_tensor_tensor(x[:, t, cols], x[:, t, cols], ALPHA, acc[:, t, cols],
                                         ALU.mult, ALU.add).then_inc(ln_z, 1)

            def out_group(layer, ob, t):
                g = 5 * ob + t
                cols = slice(ob * BW, (ob + 1) * BW)
                dve.wait_ge(out_mm[layer], g + 1)
                dve.tensor_tensor(acc[:, t, cols], bank(4 + g % 4, 0, BW), gate[:, 0, int(t == LAT), cols],
                                  ALU.mult).then_inc(out_ev[layer], 1)
                dve.wait_ge(out_ev[layer], g + 1)
                residual(2 * layer, t, cols)

            def down_group(layer, d, t, i=None):
                g = 5 * d + t
                dst = acc[:, t, (d % 2) * 512:(d % 2) * 512 + 512]
                dve.wait_ge(dn_mm[layer], lin(g + 1, 20, i))
                if g < 10:
                    dve.tensor_copy(dst, bank(4 + g % 4)).then_inc(acc_ok[layer], 1)
                    return
                dve.wait_ge(acc_ok[layer], lin(g - 9, 20, i))
                dve.tensor_tensor(dst, dst, bank(4 + g % 4), ALU.add).then_inc(acc_ok[layer], 1)

            def last_group(layer, d, t):
                down_group(layer, d, t)
                cols = slice((d % 2) * 512, (d % 2) * 512 + 512)
                dve.wait_ge(acc_ok[layer], 5 * d + t + 1)
                mark(dve.tensor_tensor(acc[:, t, cols], acc[:, t, cols], gate[:, 1, int(t == LAT), cols], ALU.mult))
                settle()
                residual(2 * layer + 1, t, cols)

            def norm(i, groups, need, after):
                layer, q = i // 2, 2
                if i % 2 == 1:
                    layer, q = layer + 1, 0
                for s in range(NT + 4):
                    t = s
                    if t < NT:
                        groups(t)
                        dve.wait_ge(ln_z, Z_BASE[i] + need(t))
                        if t >= 2:
                            dve.wait_ge(ln_n, NT * i + t - 1)
                        for n in range(2):
                            mark(dve.bn_stats(st[:, t % 2, 6 * n:6 * n + 6], x[:, t, n * 512:(n + 1) * 512]))
                        settle()
                        dve.bn_aggr(mv[:, t % 2, :], st[:, t % 2, :]).then_inc(ln_st, 1)
                    t = s - 1
                    if 0 <= t < NT:
                        dve.wait_ge(ln_rs, NT * i + t + 1)
                        dve.tensor_scalar(x[:, t, :], x[:, t, :], mv[:, t % 2, 0:1], rs[:, t % 2, :],
                                          ALU.subtract, ALU.mult).then_inc(ln_n, 1)
                    t = s - 2
                    if 0 <= t < NT:
                        dve.wait_ge(ln_g, NT * i + t + 1)
                        dve.tensor_tensor(x[:, t, :], x[:, t, :], gb[:, 1, :], ALU.add).then_inc(ln_x, 1)
                    if i == 3:
                        continue
                    t = s - 3
                    if 0 <= t < NT:
                        c = int(t == LAT)
                        dve.wait_ge(ln_tr, NT * i + t + 1)
                        if t >= 2:
                            dve.wait_ge(ln_lo, NT * i + t - 1)
                        for f in range(4, 8):
                            ins = dve.tensor_scalar(tmp[:, t % 2, f * P:(f + 1) * P],
                                                    bank(2 * (t % 2), f * P, (f + 1) * P),
                                                    modT[:, layer, q + 1, f, c:c + 1], modT[:, layer, q, f, c:c + 1],
                                                    ALU.mult, ALU.add)
                            if f < 7:
                                mark(ins)
                        ins.then_inc(ln_md, 1)
                    t = s - 4
                    if 0 <= t < NT:
                        dve.wait_ge(ln_hi, NT * i + t + 1)
                        dve.tensor_tensor(hlo[:, :, t * P:(t + 1) * P],
                                          tmp[:, t % 2, :].rearrange("p (f n) -> p f n", f=KT),
                                          hhi[:, :, t * P:(t + 1) * P].bitcast(F32), ALU.subtract).then_inc(ln_lo, 1)

            def square_low(layer, u, i=None):
                for m in range(2):
                    n = 2 * u + m
                    c = u // 2
                    r = tmp[:, n % 2, 0:TOK]
                    dst = 4 * (c % 2) + n % 4
                    dve.wait_ge(sq_hi[layer], lin(n + 1, 8, i))
                    dve.tensor_tensor(r, r, r, ALU.mult).then_inc(sq_f[layer], 1)
                    dve.wait_ge(sq_f[layer], lin(n + 1, 8, i))
                    dve.tensor_tensor(ulo[:, dst, :], r, uhi[:, dst, :].bitcast(F32), ALU.subtract) \
                        .then_inc(sq_lo[layer], 1)

            def mlp(layer):
                for kind, n, i in mlp_steps(dve):
                    w = w_ord[S.index((kind, layer, n))]
                    if w + 1 < len(w_k):
                        split_lo(w + 1, i)
                    if kind == "up":
                        square_low(layer, n, i)
                    elif n < 14:
                        for t in range(NT):
                            down_group(layer, n, t, i)
                    elif n == 14:
                        for t in range(NT):
                            last_group(layer, n, t)
                    else:
                        norm(2 * layer + 1, lambda t: last_group(layer, 15, t), lambda t: 6 + t, None)

            def project_out(layer):
                split_lo(W_OUT[layer])
                for ob in range(4):
                    split_lo(W_OUT[layer] + ob + 1)
                    if ob < 3:
                        for t in range(NT):
                            out_group(layer, ob, t)
                dve.wait_ge(gb_ld, 32 * (2 * layer + 1))
                norm(2 * layer, lambda t: out_group(layer, 3, t), lambda t: 16 + t, None)

            project_out(0)
            mlp(0)

            def pooled(f):
                g = f // 2
                dve.wait_ge(u_ev, f + 1)
                if f >= 2:
                    dve.wait_ge(pl_lo, f - 1)
                src = ub[:, f % 2, :]
                width, span = PADW, 1
                bufs = [pb[:, (f + 1) % 3, :], pb[:, f % 3, :]]
                for s in range(g + 1):
                    dst = bufs[(g - s + 1) % 2]
                    mark(dve.tensor_tensor(dst[:, 0:width - span], src[:, 0:width - span], src[:, span:width], ALU.add))
                    settle()
                    src, width, span = dst, width - span, 2 * span
                if f % 2 == 0:
                    dve.wait_ge(ic_ld[g % 2], 16 * (g // 2 + 1))
                w2 = POOL_W[g] // 2
                res = pb[:, f % 3, :]
                for pos, _, cnt in SEG:
                    mark(dve.tensor_tensor(res[:, pos - w2:pos - w2 + cnt], res[:, pos - w2:pos - w2 + cnt],
                                           ic[:, g % 2, pos:pos + cnt], ALU.mult))
                settle()
                for n, (pos, _, cnt) in enumerate(SEG):
                    ins = dve.tensor_tensor(res[:, pos - w2:pos - w2 + cnt], res[:, pos - w2:pos - w2 + cnt],
                                            ub[:, f % 2, pos:pos + cnt], ALU.subtract)
                    if n == 0:
                        mark(ins)
                ins.then_inc(pl_f, 1)

            def pooled_low(f):
                dve.wait_ge(pl_hi, f + 1)
                w2 = POOL_W[f // 2] // 2
                for n, (pos, t0, cnt) in enumerate(SEG):
                    ins = dve.tensor_tensor(ulo[:, f, t0:t0 + cnt], pb[:, f % 3, pos - w2:pos - w2 + cnt],
                                            uhi[:, f, t0:t0 + cnt].bitcast(F32), ALU.subtract)
                    if n == 0:
                        mark(ins)
                ins.then_inc(pl_lo, 1)

            for jb in range(4):
                split_lo(W_IN1 + jb + 1)
                for m in range(2):
                    f = 2 * jb + m
                    pooled(f)
                    if f >= 1:
                        pooled_low(f - 1)
            pooled_low(KT - 1)
            for f in range(KT):
                dve.wait_ge(px_hi, f + 1)
                dve.tensor_tensor(hlo[:, f, :], tmp[:, f % 2, 0:TOK], hhi[:, f, :].bitcast(F32), ALU.subtract) \
                    .then_inc(px_lo, 1)
            for m in range(M_MIX + SITES + 4, 48):
                mod_finish(m)
            project_out(1)
            mlp(1)


INPUTS = ["x_prompt", "x_sample", "cache_k_l0", "cache_v_l0", "state_ssm_l0", "c", "c_ctx",
          "w_mod_l0", "b_mod_l0", "w_in_l0", "conv_w_l0", "conv_b_l0", "a_log_l0", "dt_bias_l0", "d_skip_l0",
          "ssm_norm_w_l0", "lam_q1_l0", "lam_k1_l0", "lam_q2_l0", "lam_k2_l0", "subln_w_l0", "w_out_l0",
          "ln1_g_l0", "ln1_b_l0", "w_up_l0", "w_down_l0", "ln2_g_l0", "ln2_b_l0",
          "w_mod_l1", "b_mod_l1", "w_in_l1", "pool_w_l1", "pool_scale_l1", "w_out_l1",
          "ln1_g_l1", "ln1_b_l1", "w_up_l1", "w_down_l1", "ln2_g_l1", "ln2_b_l1"]
OUTPUTS = [(1, P, D), (1, LAT * P, D), (1, P, 2, NH_A, DH), (1, P, NH_A, 2 * DH), (1, 2, NH_B, 64, P)]


def kernel(**inputs):
    import concourse.bacc as bacc
    from concourse.bass_utils import run_bass_kernel_spmd

    nc = bacc.Bacc("TRN2", target_bir_lowering=False, num_devices=1)
    arrays, aps = {}, {}
    tables = dict(zip(("t_head", "t_ssd", "t_rope", "t_icnt"), shape_tables()))
    for name in INPUTS + list(tables):
        a = np.ascontiguousarray(tables[name] if name in tables else inputs[name])
        arrays[f"in_{name}"] = a
        aps[name] = nc.dram_tensor(f"in_{name}", a.shape, mybir.dt.from_np(a.dtype), kind="ExternalInput").ap()
    outs = [nc.dram_tensor(f"out_{i}", s, F32, kind="ExternalOutput").ap() for i, s in enumerate(OUTPUTS)]
    build(nc, aps, outs)
    r = run_bass_kernel_spmd(nc, [arrays], core_ids=[0])
    return tuple(r.results[0][f"out_{i}"] for i in range(len(OUTPUTS)))
```
